# Optimizing a Trainium2 kernel written in Bass

```python
import jax, jax.numpy as jnp
from jax import lax
import numpy as np

D_MODEL = 1024
BATCH = 1
SEQ = 512
DEPTH = 2

CHUNK = 64
HEAD_DIM = 64
A_HEADS = 8
A_LEFT_CHUNKS = 8
A_BAND = (A_LEFT_CHUNKS + 1) * CHUNK
REL_CLIP = 128
A_WIDTH = A_HEADS * HEAD_DIM
B_HEADS = 8
B_KV_HEADS = 2
B_WINDOW = 128
B_LEFT_CHUNKS = B_WINDOW // CHUNK - 1
B_BAND = (B_LEFT_CHUNKS + 1) * CHUNK
B_WIDTH = B_HEADS * HEAD_DIM
B_KV_WIDTH = B_KV_HEADS * HEAD_DIM
N_BRANCHES = 2
IN_COLS = 3 * A_WIDTH + B_WIDTH + 2 * B_KV_WIDTH + N_BRANCHES * D_MODEL
D_FF = 2816
N_EXPERTS = 8
TOP_K = 2
D_FF_EXPERT = 1408
N_DENSE = (DEPTH + 1) // 2
N_MOE = DEPTH // 2
EPS = 1e-6
NEG_INF = -1e30

kernel_name = "hybrid_chunk_relpos_swa_sink_moe"

def rmsnorm(x, g):
    xf = x.astype(jnp.float32)
    y = xf * lax.rsqrt(jnp.mean(xf * xf, axis=-1, keepdims=True) + EPS)
    return (y * g.astype(jnp.float32)).astype(x.dtype)

def band_gather(t, n_left):
    nc = t.shape[1]
    tp = jnp.pad(t, ((0, 0), (n_left, 0), (0, 0), (0, 0), (0, 0)))
    return jnp.concatenate([tp[:, i:i + nc] for i in range(n_left + 1)], axis=2)

def band_valid(nc, n_left, band):
    key_chunk = jnp.arange(nc)[:, None] + (jnp.arange(band) // CHUNK)[None, :] - n_left
    return key_chunk >= 0

def chunk_relpos_attention(q, k, v, rel_bias):
    b, s, h, d = q.shape
    nc = s // CHUNK
    qc = q.reshape(b, nc, CHUNK, h, d)
    kb = band_gather(k.reshape(b, nc, CHUNK, h, d), A_LEFT_CHUNKS)
    vb = band_gather(v.reshape(b, nc, CHUNK, h, d), A_LEFT_CHUNKS)
    scores = jnp.einsum('bnqhd,bnkhd->bnhqk', qc, kb,
                        preferred_element_type=jnp.float32) * (d ** -0.5)
    dist = jnp.arange(CHUNK)[:, None] + A_LEFT_CHUNKS * CHUNK - jnp.arange(A_BAND)[None, :]
    idx = jnp.clip(dist, -REL_CLIP, REL_CLIP) + REL_CLIP
    bias = rel_bias.astype(jnp.float32)[:, idx]
    valid = band_valid(nc, A_LEFT_CHUNKS, A_BAND)
    scores = jnp.where(valid[None, :, None, None, :], scores + bias[None, None], NEG_INF)
    probs = jax.nn.softmax(scores, axis=-1)
    out = jnp.einsum('bnhqk,bnkhd->bnqhd', probs.astype(v.dtype), vb)
    return out.reshape(b, s, h * d)

def swa_sink_alibi_attention(q, k, v, sinks):
    b, s, hq, d = q.shape
    hkv = k.shape[2]
    g = hq // hkv
    nc = s // CHUNK
    qc = q.reshape(b, nc, CHUNK, hkv, g, d)
    kb = band_gather(k.reshape(b, nc, CHUNK, hkv, d), B_LEFT_CHUNKS)
    vb = band_gather(v.reshape(b, nc, CHUNK, hkv, d), B_LEFT_CHUNKS)
    scores = jnp.einsum('bnqhgd,bnkhd->bnhgqk', qc, kb,
                        preferred_element_type=jnp.float32) * (d ** -0.5)
    slopes = jnp.exp2(-8.0 * jnp.arange(1, hq + 1, dtype=jnp.float32) / hq).reshape(hkv, g)
    dist = (jnp.arange(CHUNK)[:, None] + B_LEFT_CHUNKS * CHUNK
            - jnp.arange(B_BAND)[None, :]).astype(jnp.float32)
    alibi = -slopes[:, :, None, None] * jnp.abs(dist)[None, None]
    valid = band_valid(nc, B_LEFT_CHUNKS, B_BAND)
    scores = jnp.where(valid[None, :, None, None, None, :], scores + alibi[None, None], NEG_INF)
    sink = sinks.astype(jnp.float32).reshape(hkv, g)[None, None, :, :, None, None]
    m = jnp.maximum(jnp.max(scores, axis=-1, keepdims=True), sink)
    e = jnp.exp(scores - m)
    probs = e / (jnp.sum(e, axis=-1, keepdims=True) + jnp.exp(sink - m))
    out = jnp.einsum('bnhgqk,bnkhd->bnqhgd', probs.astype(v.dtype), vb)
    return out.reshape(b, s, hq * d)

def swiglu(h, w_gate, w_up, w_down):
    return (jax.nn.silu(h @ w_gate) * (h @ w_up)) @ w_down

def moe_swiglu(h, w_router, w_gate, w_up, w_down):
    logits = (h @ w_router).astype(jnp.float32)
    top_v, top_i = lax.top_k(logits, TOP_K)
    top_w = jax.nn.softmax(top_v, axis=-1)
    combine = jnp.sum(jax.nn.one_hot(top_i, N_EXPERTS, dtype=jnp.float32)
                      * top_w[..., None], axis=-2).astype(h.dtype)
    out = jnp.zeros_like(h)
    for e in range(N_EXPERTS):
        out = out + combine[..., e:e + 1] * swiglu(h, w_gate[e], w_up[e], w_down[e])
    return out

def mixer_block(h, w_in, b_gate, rel_bias, sinks, w_branch_a, w_branch_b, w_out):
    b, s, _ = h.shape
    proj = h @ w_in
    offs = [int(o) for o in np.cumsum([A_WIDTH, A_WIDTH, A_WIDTH, B_WIDTH, B_KV_WIDTH, B_KV_WIDTH])]
    qa, ka, va, qb, kb, vb, gate_logits = jnp.split(proj, offs, axis=-1)
    ya = chunk_relpos_attention(qa.reshape(b, s, A_HEADS, HEAD_DIM),
                                ka.reshape(b, s, A_HEADS, HEAD_DIM),
                                va.reshape(b, s, A_HEADS, HEAD_DIM), rel_bias)
    yb = swa_sink_alibi_attention(qb.reshape(b, s, B_HEADS, HEAD_DIM),
                                  kb.reshape(b, s, B_KV_HEADS, HEAD_DIM),
                                  vb.reshape(b, s, B_KV_HEADS, HEAD_DIM), sinks)
    gates = jax.nn.sigmoid(gate_logits.astype(jnp.float32) + b_gate.astype(jnp.float32))
    gates = gates.reshape(b, s, N_BRANCHES, D_MODEL).astype(h.dtype)
    merged = gates[:, :, 0] * (ya @ w_branch_a) + gates[:, :, 1] * (yb @ w_branch_b)
    return merged @ w_out

def setup_inputs(seed: int = 0) -> dict:
    key = jax.random.key(seed)
    ks = jax.random.split(key, 20)

    def nrm(k, shape, scale):
        return jax.random.normal(k, shape, jnp.float32) * scale

    return {
        "x": nrm(ks[0], (BATCH, SEQ, D_MODEL), 1.0),
        "norm_mix": 1.0 + nrm(ks[1], (DEPTH, D_MODEL), 0.05),
        "w_in": nrm(ks[2], (DEPTH, D_MODEL, IN_COLS), D_MODEL ** -0.5),
        "b_gate": nrm(ks[3], (DEPTH, N_BRANCHES * D_MODEL), 0.1),
        "rel_bias": nrm(ks[4], (DEPTH, A_HEADS, 2 * REL_CLIP + 1), 0.1),
        "sinks": nrm(ks[5], (DEPTH, B_HEADS), 0.5),
        "w_branch_a": nrm(ks[6], (DEPTH, A_WIDTH, D_MODEL), A_WIDTH ** -0.5),
        "w_branch_b": nrm(ks[7], (DEPTH, B_WIDTH, D_MODEL), B_WIDTH ** -0.5),
        "w_out": nrm(ks[8], (DEPTH, D_MODEL, D_MODEL), D_MODEL ** -0.5),
        "norm_ffn": 1.0 + nrm(ks[9], (DEPTH, D_MODEL), 0.05),
        "ffn_w_gate": nrm(ks[10], (N_DENSE, D_MODEL, D_FF), D_MODEL ** -0.5),
        "ffn_w_up": nrm(ks[11], (N_DENSE, D_MODEL, D_FF), D_MODEL ** -0.5),
        "ffn_w_down": nrm(ks[12], (N_DENSE, D_FF, D_MODEL), D_FF ** -0.5),
        "w_router": nrm(ks[13], (N_MOE, D_MODEL, N_EXPERTS), D_MODEL ** -0.5),
        "moe_w_gate": nrm(ks[14], (N_MOE, N_EXPERTS, D_MODEL, D_FF_EXPERT), D_MODEL ** -0.5),
        "moe_w_up": nrm(ks[15], (N_MOE, N_EXPERTS, D_MODEL, D_FF_EXPERT), D_MODEL ** -0.5),
        "moe_w_down": nrm(ks[16], (N_MOE, N_EXPERTS, D_FF_EXPERT, D_MODEL), D_FF_EXPERT ** -0.5),
        "norm_final": 1.0 + nrm(ks[17], (D_MODEL,), 0.05),
    }

def reference(x, norm_mix, w_in, b_gate, rel_bias, sinks, w_branch_a, w_branch_b, w_out,
              norm_ffn, ffn_w_gate, ffn_w_up, ffn_w_down, w_router, moe_w_gate, moe_w_up,
              moe_w_down, norm_final):
    for layer in range(DEPTH):
        h = rmsnorm(x, norm_mix[layer])
        x = x + mixer_block(h, w_in[layer], b_gate[layer], rel_bias[layer], sinks[layer],
                            w_branch_a[layer], w_branch_b[layer], w_out[layer])
        h = rmsnorm(x, norm_ffn[layer])
        j = layer // 2
        if layer % 2 == 0:
            x = x + swiglu(h, ffn_w_gate[j], ffn_w_up[j], ffn_w_down[j])
        else:
            x = x + moe_swiglu(h, w_router[j], moe_w_gate[j], moe_w_up[j], moe_w_down[j])
    return rmsnorm(x, norm_final)


_drawn_inputs = setup_inputs


def setup_inputs(seed=0):
    import zlib

    import numpy as np

    out = dict(_drawn_inputs(seed))
    spreads = {}
    factors = {'b_gate': 3.989, 'rel_bias': 2.921, 'sinks': 3.804}
    for name, (base, spread) in spreads.items():
        noise = np.random.default_rng([zlib.crc32(name.encode()), seed]).standard_normal(out[name].shape)
        drawn = base * np.exp(spread * noise) if base else spread * noise
        out[name] = __import__('jax').numpy.asarray(drawn.astype(out[name].dtype))
    for name, factor in factors.items():
        out[name] = (out[name] * factor).astype(out[name].dtype)
    return out
```

```python
from contextlib import ExitStack

import concourse.bass as bass
from concourse import mybir

F32 = mybir.dt.float32
F32R = mybir.dt.float32r
BF16 = mybir.dt.bfloat16
U32 = mybir.dt.uint32
I32 = mybir.dt.int32
ALU = mybir.AluOpType
ACT = mybir.ActivationFunctionType
AX = mybir.AxisListType

P = 128
D = 1024
T = 512
DEPTH = 2
KD = D // P
TT = T // P
HEADS = 8
HD = 64
D_FF = 2816
KF = D_FF // P
REL = 128
EPS = 1e-6
SCALE = HD ** -0.5
MASKED = -1e30

UNIT = 8 * P
RAW = 4
SPL = 2

N_PROJ, N_V, N_GATE, N_BR, N_OUT = 13, 5, 16, 8, 8
U_V = N_PROJ
U_GATE = U_V + N_V
U_BR = U_GATE + N_GATE
U_OUT = U_BR + N_BR
N_MIX = U_OUT + N_OUT
N_GU = 2 * KF
DOWN_TILES = (8, 8, 6)
N_DOWN = 3 * KD
N_FFN = N_GU + N_DOWN
MIX_START = (0, N_MIX + N_FFN)
FFN_START = N_MIX
STEPS = 2 * HEADS * TT

U_ROUTER = MIX_START[1] + N_MIX
EXPERTS = 8
D_FFE = 1408
KFE = D_FFE // P
CHUNKS = (4, 4, 3)
M_RAW, M_SPL = 7, 5
M_UNITS = 8 * len(CHUNKS) + KFE
SLOTS = 2
CAP = SLOTS * P
HALVES = T // CAP
LISTS = HALVES * EXPERTS * SLOTS
PAD_H, PAD_Y = T, 2 * T


def build_kernel(nc, xT, g_mix, w_in, b_gate, rel_ext, sinks, w_a, w_b, w_out, g_ffn, w_gu, w_down, w_router,
                 moe_gu, moe_down, g_ffn_row, g_final_row, out):
    ctx = ExitStack()
    with ctx:
        def sb(name, shape, dt=F32, where=ctx):
            return where.enter_context(nc.sbuf_tensor(name, shape, dt))

        def sem(name):
            return ctx.enter_context(nc.semaphore(name))

        norm = sb("norm", [P, T])
        ident = sb("ident", [P, P])
        ones = sb("ones", [P, P])
        eps = sb("eps", [P, 1])
        gains = sb("gains", [P, 2 * DEPTH, KD])

        dense = ExitStack()
        xs = sb("xs", [P, KD, T], F32, dense)
        h_hi = sb("h_hi", [P, KD, T], F32R, dense)
        h_lo = sb("h_lo", [P, KD, T], F32R, dense)
        raw = sb("raw", [P, RAW, UNIT], F32, dense)
        w_hi = sb("w_hi", [P, SPL, UNIT], F32R, dense)
        w_lo = sb("w_lo", [P, SPL, UNIT], F32R, dense)

        attn = ExitStack()
        gates = sb("gates", [P, N_GATE, T], F32, attn)
        kq_hi = sb("kq_hi", [P, N_PROJ, T], F32R, attn)
        kq_lo = sb("kq_lo", [P, N_PROJ, T], F32R, attn)
        v_hi = sb("v_hi", [P, TT, N_V * P], F32R, attn)
        v_lo = sb("v_lo", [P, TT, N_V * P], F32R, attn)
        probs = sb("probs", [P, 2, T], F32, attn)
        pT_hi = sb("pT_hi", [P, 2, T], F32R, attn)
        pT_lo = sb("pT_lo", [P, 2, T], F32R, attn)
        bias = sb("bias", [P, 2 * P], F32, attn)
        bias_hi = sb("bias_hi", [P, 2, 2 * P], F32R, attn)
        bias_lo = sb("bias_lo", [P, 2, 2 * P], F32R, attn)
        flip = sb("flip", [P, P], F32, attn)
        flip_r = sb("flip_r", [P, P], F32R, attn)
        far_hi = sb("far_hi", [P, DEPTH, HEADS], F32R, attn)
        far_lo = sb("far_lo", [P, DEPTH, HEADS], F32R, attn)
        alibi = sb("alibi", [P, 2 * P], F32, attn)
        far = sb("far", [P, DEPTH, HEADS], F32, attn)
        sink = sb("sink", [P, DEPTH, HEADS], F32, attn)
        nsink = sb("nsink", [P, DEPTH, HEADS], F32, attn)
        bg = sb("bg", [P, DEPTH, N_GATE], F32, attn)
        stat = sb("stat", [P, 6, 4], F32, attn)
        attn.close()

        ffn = ExitStack()
        a_hi = sb("a_hi", [P, KF, T], F32R, ffn)
        a_lo = sb("a_lo", [P, KF, T], F32R, ffn)
        silu = sb("silu", [P, 2, T], F32, ffn)
        act = sb("act", [P, 2, T], F32, ffn)
        ffn.close()

        routed = ExitStack()
        m_raw = sb("m_raw", [P, M_RAW, UNIT], F32, routed)
        m_hi = sb("m_hi", [P, M_SPL, UNIT], F32R, routed)
        m_lo = sb("m_lo", [P, M_SPL, UNIT], F32R, routed)
        x_rows = sb("x_rows", [P, TT, D], F32, routed)
        h_rows = sb("h_rows", [P, 2, D], F32, routed)
        g_row = sb("g_row", [P, D], F32, routed)
        rt = sb("rt", [P, 12, TT, EXPERTS], F32, routed)
        r1 = sb("r1", [P, 12, TT], F32, routed)
        picks = sb("picks", [P, TT, EXPERTS], BF16, routed)
        before = sb("before", [P, P], BF16, routed)
        all_ones = sb("all_ones", [P, P], BF16, routed)
        place = sb("place", [P, TT, 2], U32, routed)
        entry = sb("entry", [P, TT, 2, 2], U32, routed)
        lists = sb("lists", [P, LISTS, 2], U32, routed)
        counts = sb("counts", [P, EXPERTS], I32, routed)
        most = sb("most", [P, 1], I32, routed)
        routed.close()
        dense.close()

        expert = ExitStack()
        xg = sb("xg", [P, SLOTS, D], F32, expert)
        xt_hi = sb("xt_hi", [P, KD, SLOTS, P], F32R, expert)
        xt_lo = sb("xt_lo", [P, KD, SLOTS, P], F32R, expert)
        m_silu = sb("m_silu", [P, SLOTS, T], F32, expert)
        m_act = sb("m_act", [P, SLOTS, T], F32, expert)
        at_hi = sb("at_hi", [P, KFE, SLOTS, P], F32R, expert)
        at_lo = sb("at_lo", [P, KFE, SLOTS, P], F32R, expert)
        y_stage = sb("y_stage", [P, SLOTS, D], F32, expert)
        y_in = sb("y_in", [P, 2, 2, D], F32, expert)
        expert.close()
        logits_T = y_in[:, 0, 0, 0:T]
        gf_row = h_rows[:, 0, :]

        h_dram = nc.dram_tensor("h_dram", [T + 1, D], F32, kind="Internal").ap()
        y_dram = nc.dram_tensor("y_dram", [2 * T, D], F32, kind="Internal").ap()
        list_dram = nc.dram_tensor("list_dram", [P * LISTS, 2], U32, kind="Internal").ap()

        ps = ctx.enter_context(nc.psum_tensor("ps", [P, 8, T], F32))
        S_BANK, T_BANK, O_BANK, SUM_BANK = 2, 4, 6, 7
        SQ_BANK, H32_BANK = 2, 4

        raw_full = [sem(f"raw_full{i}") for i in range(RAW)]
        hi_ready, lo_ready = sem("hi_ready"), sem("lo_ready")
        unit_done = sem("unit_done")
        small_in = sem("small_in")
        x_in = sem("x_in")
        consts = sem("consts")
        const_step = sem("const_step")
        drained_act, drained_dve = sem("drained_act"), sem("drained_dve")
        x_updated, squared, summed = sem("x_updated"), sem("squared"), sem("summed")
        sum_bcast, rms_base, rms_ready = sem("sum_bcast"), sem("rms_base"), sem("rms_ready")
        h32_ready, h_hi_ready, h_lo_ready = sem("h32_ready"), sem("h_hi_ready"), sem("h_lo_ready")
        kq_hi_ready = sem("kq_hi_ready")
        vT_copied, vT_turned, v_hi_ready, v_lo_ready = sem("vT_copied"), sem("vT_turned"), sem("v_hi_ready"), sem("v_lo_ready")
        bias_in, bias_masked, bias_hi_ready, bias_lo_ready = sem("bias_in"), sem("bias_masked"), sem("bias_hi_ready"), sem("bias_lo_ready")
        far_hi_ready, flip_ready = sem("far_hi_ready"), sem("flip_ready")
        scores_ready, max_ready, nmax_ready = sem("scores_ready"), sem("max_ready"), sem("nmax_ready")
        sink_exp, exp_ready, denom, rcp_ready, probs_ready = sem("sink_exp"), sem("exp_ready"), sem("denom"), sem("rcp_ready"), sem("probs_ready")
        pT_ready, pT_hi_ready, pT_lo_ready, pv_done = sem("pT_ready"), sem("pT_hi_ready"), sem("pT_lo_ready"), sem("pv_done")
        y_hi_ready, y_lo_ready = sem("y_hi_ready"), sem("y_lo_ready")
        gated, merged32, merged_hi, merged_lo = sem("gated"), sem("merged32"), sem("merged_hi"), sem("merged_lo")
        silu_ready, act_ready, a_hi_ready, a_lo_ready = sem("silu_ready"), sem("act_ready"), sem("a_hi_ready"), sem("a_lo_ready")
        out_sent = sem("out_sent")

        m_full = [sem(f"m_full{i}") for i in range(M_RAW)]
        m_hi_ready, m_lo_ready, m_done = sem("m_hi_ready"), sem("m_lo_ready"), sem("m_done")
        rinv_turned, rinv_ready = sem("rinv_turned"), sem("rinv_ready")
        x_turned, x_copied = sem("x_turned"), sem("x_copied")
        logits_ready, logits_turned = sem("logits_ready"), sem("logits_turned")
        gap_ready, gap_exp = sem("gap_ready"), sem("gap_exp")
        route_consts, route_step, picks_ready, ranks_ready = sem("route_consts"), sem("route_step"), sem("picks_ready"), sem("ranks_ready")
        pads_sent, places_ready, entries_sent, lists_in, counts_ready = sem("pads_sent"), sem("places_ready"), sem("entries_sent"), sem("lists_in"), sem("counts_ready")
        pool_step = sem("pool_step")
        rows_in, h_row_ready = sem("rows_in"), sem("h_row_ready")
        h_row_sent = [sem("h_row_sent0"), sem("h_row_sent1")]
        xg_in = [sem("xg_in0"), sem("xg_in1")]
        xt_turned, xt_hi_ready, xt_lo_ready = sem("xt_turned"), sem("xt_hi_ready"), sem("xt_lo_ready")
        m_silu_ready, m_act_ready = sem("m_silu_ready"), sem("m_act_ready")
        at_turned, at_hi_ready, at_lo_ready = sem("at_turned"), sem("at_hi_ready"), sem("at_lo_ready")
        y_copied = sem("y_copied")
        y_sent = [sem("y_sent0"), sem("y_sent1")]
        stage_free = sem("stage_free")
        moe_done = sem("moe_done")
        y_back = [sem("y_back0"), sem("y_back1")]
        mixed, mix_step, sq_ready, root_ready, inv_ready, out_ready = sem("mixed"), sem("mix_step"), sem("sq_ready"), sem("root_ready"), sem("inv_ready"), sem("out_ready")

        N_SMALL = 7

        def expert_units():
            for c, nb in enumerate(CHUNKS):
                for what in ("gate", "up"):
                    for j in range(4):
                        yield what, c, j, 2 * nb * P
            for f in range(KFE):
                yield "down", 0, f, D

        UNITS = list(expert_units())
        assert len(UNITS) == M_UNITS and M_UNITS % M_RAW == 0 and M_UNITS % M_SPL == 0
        CHUNK_END = {c: {w: max(u for u, x in enumerate(UNITS) if x[0] == w and x[1] == c) for w in ("gate", "up")}
                     for c in range(len(CHUNKS))}
        Y_BANKS = (6, 2)
        DOWN0 = M_UNITS - KFE
        TURN_LAST, TURN_X = DOWN0 + 1, (DOWN0 + 3, DOWN0 + 6)
        TURNED_AT = {CHUNK_END[0]["up"] + 1: 0, CHUNK_END[1]["up"] + 1: 1, TURN_LAST: 2}
        N_SEC = EXPERTS

        def step(s):
            hh, qb = s // TT, s % TT
            if hh < HEADS:
                return dict(hh=hh, qb=qb, a=True, q=4 + hh // 2, k=hh // 2, rows=HD * (hh % 2), v=hh // 2,
                            k0=0, nk=(qb + 1) * P)
            j, g = (hh - HEADS) // 2, hh % 2
            k0 = max(qb - 1, 0) * P
            return dict(hh=hh, qb=qb, a=False, q=8 + j, k=12, rows=HD * g, v=4, head=j + 4 * g,
                        k0=k0, nk=(qb + 1) * P - k0)

        def branch_banks(i):
            return (2, 4) if i % 2 == 0 else (6, 0)

        GATES_AT = {4 * g: g for g in range(N_GATE)}
        NORMS = 2 * DEPTH

        block = ctx.enter_context(nc.Block())

        @block.sync
        def _(sp):
            for k in range(KD):
                sp.dma_start(xs[:, k, :], xT[:, k, :]).then_inc(x_in, 16)
            sp.dma_start(gains[:, 0:DEPTH, :], g_mix).then_inc(small_in, 16)
            sp.dma_start(gains[:, DEPTH:2 * DEPTH, :], g_ffn).then_inc(small_in, 16)
            sp.dma_start(bg[:], b_gate).then_inc(small_in, 16)
            for layer in range(DEPTH):
                sp.dma_start(sink[:, layer, :], bass.AP(tensor=sinks.tensor, offset=layer * HEADS, ap=[[0, P], [1, HEADS]])).then_inc(small_in, 16)
                sp.dma_start(far[:, layer, :], bass.AP(tensor=rel_ext.tensor, offset=layer * HEADS * 384,
                                                       ap=[[0, P], [384, HEADS]]), allow_slow_non_contiguous=True).then_inc(small_in, 16)

            def load(n, src):
                if n >= RAW:
                    sp.wait_ge(lo_ready, n - RAW + 1)
                sp.dma_start(raw[:, n % RAW, 0:src.shape[1]], src).then_inc(raw_full[n % RAW], 16)

            for layer in range(DEPTH):
                n = MIX_START[layer]
                for u in range(U_BR):
                    load(n + u, w_in[layer, u])
                for i in range(N_BR // 2):
                    load(n + U_BR + 2 * i, w_a[layer, i])
                    load(n + U_BR + 2 * i + 1, w_b[layer, i])
                for u in range(N_OUT):
                    load(n + U_OUT + u, w_out[layer, u])
                if layer == 0:
                    for u in range(N_GU):
                        load(FFN_START + u, w_gu[u])
                    for u in range(N_DOWN):
                        c = 8 * (u % 3) * P
                        load(FFN_START + N_GU + u, w_down[u // 3, :, c:c + DOWN_TILES[u % 3] * P])
            load(U_ROUTER, w_router)
            sp.wait_ge(x_updated, 3 * KD)
            sp.dma_start(g_row[:], bass.AP(tensor=g_ffn_row.tensor, offset=0, ap=[[0, P], [1, D]])).then_inc(rows_in, 16)

            def expert_unit(e, u):
                what, c, j, cols = UNITS[u % M_UNITS]
                src = moe_down if what == "down" else moe_gu[c]
                row = j if what == "down" else 4 * (what == "up") + j
                sp.dma_start(m_raw[:, u % M_RAW, 0:cols], src[bass.ds(e, 1), row, :, :].rearrange("e p c -> p (e c)")
                             ).then_inc(m_full[u % M_RAW], 16)

            for u in range(M_RAW):
                expert_unit(0, u)

            def weights(first):
                with sp.Fori(0, N_SEC) as i:
                    following = (i + 1) % EXPERTS
                    for u in range(M_UNITS):
                        sp.wait_ge(m_lo_ready, i * M_UNITS + (first * M_UNITS + u + 1))
                        expert_unit(i if u + M_RAW < M_UNITS else following, u + M_RAW)

            weights(0)
            sp.wait_ge(h_row_sent[0], 16 * 3)
            sp.dma_start(gf_row, bass.AP(tensor=g_final_row.tensor, offset=0, ap=[[0, P], [1, D]])).then_inc(rows_in, 16)
            sp.wait_ge(counts_ready, 1)
            with sp.If(sp.value_load(most[0:1, 0:1], min_val=0, max_val=T) > CAP):
                weights(N_SEC)
            sp.wait_ge(moe_done, 1)
            for t in range(TT):
                if t >= 2:
                    sp.wait_ge(mixed, t - 1)
                sp.dma_start(y_in[:, t % 2, :, :], y_dram[2 * t * P:2 * (t + 1) * P, :].rearrange("(p c) d -> p c d", c=2)
                             ).then_inc(y_back[t % 2], 16)
            for t in range(TT):
                sp.wait_ge(out_ready, t + 1)
                sp.dma_start(out[t * P:(t + 1) * P, :], x_rows[:, t, :]).then_inc(out_sent, 16)
            sp.wait_ge(out_sent, 16 * TT)

        @block.gpsimd
        def _(pool):
            pool.memset(ident[:], 0.0).then_inc(const_step, 1)
            pool.memset(ones[:], 1.0 / D).then_inc(consts, 1)
            pool.wait_ge(const_step, 1)
            pool.affine_select(out=ident[:], in_=ident[:], compare_op=ALU.not_equal, fill=1.0, base=0,
                               pattern=[[-1, P]], channel_multiplier=1).then_inc(consts, 1)
            pool.memset(flip[:], 0.0).then_inc(const_step, 1)
            pool.wait_ge(const_step, 2)
            pool.affine_select(out=flip[:], in_=flip[:], compare_op=ALU.not_equal, fill=1.0, base=1 - P,
                               pattern=[[1, P]], channel_multiplier=1).then_inc(consts, 1)
            pool.iota(alibi[:], [[-1, 2 * P]], base=2 * P - 1, channel_multiplier=-1,
                      allow_small_or_imprecise_dtypes=True).then_inc(const_step, 1)
            pool.wait_ge(const_step, 3)
            pool.memset(alibi[0:HD, 0:2 * HD], -MASKED).then_inc(const_step, 1)
            pool.wait_ge(const_step, 4)
            pool.memset(alibi[HD:P, 0:HD], -MASKED).then_inc(const_step, 1)
            pool.wait_ge(const_step, 5)
            pool.memset(alibi[HD:P, 3 * HD:4 * HD], -MASKED).then_inc(const_step, 1)
            pool.wait_ge(const_step, 6)
            pool.sem_inc(consts, 1)
            for i in range(DEPTH * HEADS):
                if i:
                    pool.wait_ge(bias_lo_ready, i)
                pool.dma_start(bias[:], bass.AP(tensor=rel_ext.tensor, offset=i * 384, ap=[[1, P], [1, 2 * P]])).then_inc(bias_in, 16)
                pool.wait_ge(bias_in, 16 * (i + 1))
                pool.memset(bias[HD:P, 3 * HD:4 * HD], MASKED).then_inc(bias_masked, 1)
            steps = [0]

            def one(ins):
                steps[0] += 1
                ins.then_inc(pool_step, 1)
                pool.wait_ge(pool_step, steps[0])

            pool.wait_ge(bias_masked, DEPTH * HEADS)
            pool.wait_ge(x_updated, 3 * KD)
            one(pool.memset(lists[:, :, 0], PAD_H))
            one(pool.memset(lists[:, :, 1], PAD_Y))
            pool.dma_start(list_dram.rearrange("(p c) i -> p (c i)", p=P), lists[:].rearrange("p c i -> p (c i)")
                           ).then_inc(pads_sent, 16)
            one(pool.memset(all_ones[:], 1.0))
            one(pool.memset(before[:], 1.0))
            one(pool.affine_select(out=before[:], in_=before[:], compare_op=ALU.is_gt, fill=0.0, base=0,
                                   pattern=[[1, P]], channel_multiplier=-1))
            one(pool.iota(rt[:, 0, :, :], [[0, TT], [-1, EXPERTS]], base=EXPERTS, channel_multiplier=0,
                          allow_small_or_imprecise_dtypes=True))
            one(pool.iota(rt[:, 1, :, :], [[0, TT], [SLOTS, EXPERTS]], base=0, channel_multiplier=0,
                          allow_small_or_imprecise_dtypes=True))
            one(pool.iota(entry[:, :, 0, 0], [[P, TT]], base=0, channel_multiplier=1))
            one(pool.iota(entry[:, :, 1, 0], [[P, TT]], base=0, channel_multiplier=1))
            one(pool.iota(entry[:, :, 0, 1], [[2 * P, TT]], base=0, channel_multiplier=2))
            one(pool.iota(entry[:, :, 1, 1], [[2 * P, TT]], base=1, channel_multiplier=2))
            pool.sem_inc(route_consts, 1)
            one(pool.memset(h_rows[0:1, 0, :], 0.0))
            pool.dma_start(h_dram[T:T + 1, :], h_rows[0:1, 0, :]).then_inc(h_row_sent[0], 16)
            pool.wait_ge(h_row_sent[0], 16)
            pool.sem_inc(route_consts, 1)
            pool.wait_ge(pads_sent, 16)
            pool.wait_ge(places_ready, 1)
            for t in range(TT):
                for c in range(2):
                    pool.indirect_dma_start(out=list_dram, out_offset=bass.IndirectOffsetOnAxis(ap=place[:, t, c:c + 1], axis=0),
                                            in_=entry[:, t, c, :], in_offset=None).then_inc(entries_sent, 16)
            for t in range(TT):
                pool.wait_ge(h_row_ready, t + 1)
                pool.dma_start(h_dram[t * P:(t + 1) * P, :], h_rows[:, t % 2, :]).then_inc(h_row_sent[t % 2], 16)
            pool.wait_ge(entries_sent, 16 * 2 * TT)
            pool.dma_start(lists[:].rearrange("p c i -> p (c i)"), list_dram.rearrange("(p c) i -> p (c i)", p=P)
                           ).then_inc(lists_in, 16)
            pool.wait_ge(lists_in, 16)
            pool.wait_ge(h_row_sent[0], 16 * 3)
            pool.wait_ge(h_row_sent[1], 16 * 2)

            def gather(p):
                for sl in range(SLOTS):
                    pool.indirect_dma_start(out=xg[:, sl, :], out_offset=None, in_=h_dram,
                                            in_offset=bass.IndirectOffsetOnAxis(ap=lists[:, SLOTS * p + sl, 0:1], axis=0)
                                            ).then_inc(xg_in[sl], 16)

            def moves(first):
                for p in range(first, first + N_SEC):
                    for sl in range(SLOTS):
                        pool.wait_ge(xg_in[sl], 16 * (p + 2))
                    pool.wait_ge(xt_turned, 4 * (p + 2))
                    gather(min(p + 2, 2 * N_SEC - 1))
                    for sl in range(SLOTS):
                        if p:
                            pool.wait_ge(y_sent[sl], 16 * p)
                        pool.sem_inc(stage_free, 1)
                    for sl in range(SLOTS):
                        pool.wait_ge(y_copied, SLOTS * p + SLOTS + sl + 1)
                        pool.indirect_dma_start(out=y_dram, out_offset=bass.IndirectOffsetOnAxis(ap=lists[:, SLOTS * p + sl, 1:2], axis=0),
                                                in_=y_stage[:, sl, :], in_offset=None, bounds_check=2 * T - 1,
                                                oob_is_err=False).then_inc(y_sent[sl], 16)
                for sl in range(SLOTS):
                    pool.wait_ge(y_sent[sl], 16 * (first + N_SEC))
                    pool.wait_ge(xg_in[sl], 16 * (first + N_SEC + 2))

            gather(0)
            pool.wait_ge(xg_in[0], 16)
            pool.wait_ge(xg_in[1], 16)
            pool.wait_ge(xt_turned, 4)
            gather(1)
            moves(0)
            with pool.If(pool.value_load(most[0:1, 0:1], min_val=0, max_val=T) > CAP):
                moves(N_SEC)
            pool.sem_inc(moe_done, 1)

        @block.scalar
        def _(act_):
            A = act_

            def split_hi(n, cols=UNIT):
                A.wait_ge(raw_full[n % RAW], 16 * (n // RAW + 1))
                if n >= SPL:
                    A.wait_ge(unit_done, n - SPL + 1)
                A.activation(w_hi[:, n % SPL, 0:cols], raw[:, n % RAW, 0:cols], ACT.Copy).then_inc(hi_ready, 1)

            def square(i, k):
                if i < KD:
                    A.wait_ge(x_in, 16 * KD)
                else:
                    A.wait_ge(x_updated, i - KD + 1)
                if i >= 2:
                    A.wait_ge(summed, i - 1)
                A.activation(ps[:, SQ_BANK + i % 2, :], xs[:, k, :], ACT.Square).then_inc(squared, 1)

            def root(j):
                A.wait_ge(sum_bcast, j + 1)
                A.activation(norm[:], ps[:, SUM_BANK, :], ACT.Sqrt, bias=eps[:, 0:1]).then_inc(rms_base, 1)

            def bias_split(H):
                layer, hh = H // (2 * HEADS), H % (2 * HEADS)
                if H >= 2:
                    A.wait_ge(scores_ready, TT * (H - 1))
                if hh < HEADS:
                    A.wait_ge(bias_masked, layer * HEADS + hh + 1)
                    A.activation(bias_hi[:, H % 2, :], bias[:], ACT.Copy).then_inc(bias_hi_ready, 1)
                else:
                    A.activation(bias_hi[:, H % 2, :], alibi[:], ACT.Copy,
                                 scale=-2.0 ** -(step(TT * hh)["head"] + 1)).then_inc(bias_hi_ready, 1)

            def h_split(i):
                A.wait_ge(h32_ready, i + 1)
                A.activation(h_hi[:, i % KD, :], ps[:, H32_BANK + i % 2, :], ACT.Copy).then_inc(h_hi_ready, 1)

            split_hi(0)
            split_hi(1)
            A.wait_ge(consts, 6)
            A.activation(flip_r[:], flip[:], ACT.Copy).then_inc(flip_ready, 1)
            A.activation(far_hi[:], far[:], ACT.Copy).then_inc(far_hi_ready, 1)
            for k in range(KD):
                square(k, k)
            for layer in range(DEPTH):
                n0 = MIX_START[layer]
                norm_i = 2 * layer
                root(norm_i)
                for k in range(KD):
                    h_split(norm_i * KD + k)
                for u in range(N_PROJ):
                    n = n0 + u
                    A.wait_ge(unit_done, n + 1)
                    split_hi(n + 2)
                    A.activation(kq_hi[:, u, :], ps[:, n % 2, :], ACT.Copy,
                                 scale=SCALE if 4 <= u < 12 else 1.0).then_inc(kq_hi_ready, 1)
                for u in range(N_V + 1):
                    n = n0 + U_V + u
                    if u < N_V:
                        A.wait_ge(unit_done, n + 1)
                        split_hi(n + 2)
                        i = layer * N_V + u
                        if i >= 2:
                            A.wait_ge(vT_turned, i - 1)
                        A.activation(probs[:, i % 2, :], ps[:, n % 2, :], ACT.Copy).then_inc(vT_copied, 1)
                    if u >= 1:
                        i = layer * N_V + u - 1
                        A.wait_ge(vT_turned, i + 1)
                        A.activation(v_hi[:, :, (u - 1) * P:u * P],
                                     ps[:, T_BANK + i % 2, :].rearrange("p (t c) -> p t c", c=P),
                                     ACT.Copy).then_inc(v_hi_ready, 1)

                bias_split(layer * 2 * HEADS)
                for tick in range(STEPS + 4):
                    if 2 <= tick < STEPS + 2:
                        s, st = layer * STEPS + tick - 2, step(tick - 2)
                        A.wait_ge(pT_ready, s + 1)
                        if s >= 2:
                            A.wait_ge(pv_done, s - 1)
                        A.activation(pT_hi[:, s % 2, 0:st["nk"]], ps[:, T_BANK + s % 2, 0:st["nk"]],
                                     ACT.Copy).then_inc(pT_hi_ready, 1)
                    if tick < STEPS:
                        s, st = layer * STEPS + tick, step(tick)
                        A.wait_ge(nmax_ready, s + 1)
                        c = s % 4
                        if not st["a"]:
                            A.activation(stat[:, 3, c:c + 1], sink[:, layer, st["head"]:st["head"] + 1], ACT.Exp,
                                         bias=stat[:, 1, c:c + 1]).then_inc(sink_exp, 1)
                        A.activation(probs[:, s % 2, 0:st["nk"]], ps[:, S_BANK + s % 2, 0:st["nk"]], ACT.Exp,
                                     bias=stat[:, 1, c:c + 1], accum_out=stat[:, 2, c:c + 1]).then_inc(exp_ready, 1)
                    if tick % TT == 1 and tick < STEPS - TT:
                        bias_split(layer * 2 * HEADS + tick // TT + 1)
                    if (tick - 4) in GATES_AT:
                        g = GATES_AT[tick - 4]
                        n = n0 + U_GATE + g
                        A.wait_ge(unit_done, n + 1)
                        split_hi(n + 2)
                        A.activation(gates[:, g, :], ps[:, n % 2, :], ACT.Tanh, scale=0.5,
                                     bias=bg[:, layer, g:g + 1]).then_inc(drained_act, 1)
                    if tick >= 7 and (tick - 7) % 4 == 0:
                        hh = (tick - 7) // 4
                        H = layer * 2 * HEADS + hh
                        st = step(4 * hh)
                        r = st["rows"]
                        A.wait_ge(pv_done, 4 * (H + 1))
                        A.activation(kq_hi[r:r + HD, st["q"], :], ps[r:r + HD, O_BANK + hh % 2, :],
                                     ACT.Copy).then_inc(y_hi_ready, 1)

                for i in range(N_BR // 2):
                    n = n0 + U_BR + 2 * i
                    A.wait_ge(unit_done, n + 1)
                    split_hi(n + 2)
                    A.wait_ge(unit_done, n + 2)
                    split_hi(n + 3)
                    for mm in range(2):
                        m = layer * KD + 2 * i + mm
                        A.wait_ge(merged32, m + 1)
                        A.activation(h_hi[:, 2 * i + mm, :], probs[:, 0, :], ACT.Copy, scale=0.5).then_inc(merged_hi, 1)
                last = n0 + N_MIX
                for u in range(N_OUT):
                    n = n0 + U_OUT + u
                    A.wait_ge(unit_done, n + 1)
                    if layer == 0 or n + 2 <= last:
                        split_hi(n + 2)
                    square((norm_i + 1) * KD + u, u)
                root(norm_i + 1)
                for k in range(KD):
                    h_split((norm_i + 1) * KD + k)
                if layer == 0:
                    for u in range(N_GU):
                        n = FFN_START + u
                        A.wait_ge(unit_done, n + 1)
                        split_hi(n + 2)
                        f = u // 2
                        if u % 2 == 0:
                            if f >= 2:
                                A.wait_ge(act_ready, f - 1)
                            A.activation(silu[:, f % 2, :], ps[:, n % 2, :], ACT.Silu).then_inc(silu_ready, 1)
                        else:
                            A.wait_ge(act_ready, f + 1)
                            A.activation(a_hi[:, f, :], act[:, f % 2, :], ACT.Copy).then_inc(a_hi_ready, 1)
                    for u in range(N_DOWN):
                        n = FFN_START + N_GU + u
                        A.wait_ge(unit_done, n + 1)
                        if (u + 2) % 3 == 2 and u + 2 < N_DOWN:
                            split_hi(n + 2, DOWN_TILES[2] * P)
                        else:
                            split_hi(n + 2)
                        if u % 3 == 2:
                            square(2 * KD + u // 3, u // 3)

            def x_copy(t):
                A.wait_ge(x_turned, t + 1)
                A.activation(x_rows[:, t, :], ps[:, 0:2, :].rearrange("p b c -> p (b c)"), ACT.Copy).then_inc(x_copied, 1)

            A.sem_inc(m_silu_ready, SLOTS)
            A.sem_inc(y_copied, SLOTS)
            x_copy(0)
            A.wait_ge(unit_done, U_ROUTER + 1)
            A.activation(logits_T, ps[:, 6, :], ACT.Copy).then_inc(logits_ready, 1)
            for t in range(1, TT):
                x_copy(t)
            A.wait_ge(gap_ready, 1)
            A.activation(r1[:, 3, :], r1[:, 2, :], ACT.Exp).then_inc(gap_exp, 1)

            def expert_hi(full, u):
                A.wait_ge(m_full[u % M_RAW], full)
                cols = UNITS[u % M_UNITS][3]
                A.activation(m_hi[:, u % M_SPL, 0:cols], m_raw[:, u % M_RAW, 0:cols], ACT.Copy).then_inc(m_hi_ready, 1)

            def turned_x(done, sl):
                for hb in range(2):
                    A.wait_ge(xt_turned, done + (2 * sl + hb + 1))
                    A.activation(xt_hi[:, 4 * hb:4 * hb + 4, sl, :], ps[:, hb, :].rearrange("p (k c) -> p k c", c=P),
                                 ACT.Copy).then_inc(xt_hi_ready, 1)

            for u in range(M_SPL):
                expert_hi(16, u)
            turned_x(0, 0)
            turned_x(0, 1)

            def passes(first):
                with A.Fori(0, N_SEC) as i:
                    for u in range(M_UNITS):
                        A.wait_ge(m_done, i * M_UNITS + (first * M_UNITS + u + 1))
                        v = u + M_SPL
                        expert_hi(i * (16 * (M_UNITS // M_RAW)) + 16 * (first * (M_UNITS // M_RAW) + v // M_RAW + 1), v)
                        for c in range(len(CHUNKS)):
                            if u == CHUNK_END[c]["gate"]:
                                w = CHUNKS[c] * P
                                for sl in range(SLOTS):
                                    A.wait_ge(m_act_ready, i * 6 + (6 * first + 2 * c + sl + 1))
                                    A.activation(m_silu[:, sl, 0:w], ps[:, sl, 0:w], ACT.Silu).then_inc(m_silu_ready, 1)
                        if u in TURNED_AT:
                            c = TURNED_AT[u]
                            nb = CHUNKS[c]
                            for sl in range(SLOTS):
                                A.wait_ge(at_turned, i * 6 + (6 * first + SLOTS + 2 * c + sl + 1))
                                A.activation(at_hi[:, 4 * c:4 * c + nb, sl, :],
                                             ps[:, 4 + sl, 0:nb * P].rearrange("p (k c) -> p k c", c=P),
                                             ACT.Copy).then_inc(at_hi_ready, 1)
                        if u in TURN_X:
                            turned_x(i * 4 + 4 * (first + 1), TURN_X.index(u))
                    for sl in range(SLOTS):
                        A.wait_ge(stage_free, i * SLOTS + (SLOTS * first + sl + 1))
                        A.activation(y_stage[:, sl, :], ps[:, Y_BANKS[sl]:Y_BANKS[sl] + 2, :].rearrange("p b c -> p (b c)"),
                                     ACT.Copy).then_inc(y_copied, 1)

            passes(0)
            A.wait_ge(counts_ready, 1)
            with A.If(A.value_load(most[0:1, 0:1], min_val=0, max_val=T) > CAP):
                passes(N_SEC)
            for t in range(TT):
                A.wait_ge(mixed, t + 1)
                A.activation(ps[:, 0:2, :].rearrange("p b c -> p (b c)"), x_rows[:, t, :], ACT.Square, accum_out=r1[:, 8, t:t + 1]).then_inc(sq_ready, 1)
                A.wait_ge(sq_ready, t + 1)
                A.activation(r1[:, 9, t:t + 1], r1[:, 8, t:t + 1], ACT.Sqrt, scale=1.0 / D, bias=eps[:, 0:1]).then_inc(root_ready, 1)

        @block.vector
        def _(V):
            def split_lo(n, cols=UNIT):
                V.wait_ge(hi_ready, n + 1)
                V.tensor_tensor(w_lo[:, n % SPL, 0:cols], raw[:, n % RAW, 0:cols],
                                w_hi[:, n % SPL, 0:cols].bitcast(F32), ALU.subtract).then_inc(lo_ready, 1)

            def lo_of(out, full, hi):
                return V.tensor_tensor(out, full, hi.bitcast(F32), ALU.subtract)

            def sum_squares(i, k):
                V.wait_ge(squared, i + 1)
                if k == 0:
                    if i:
                        V.wait_ge(h32_ready, i)
                    V.tensor_copy(norm[:], ps[:, SQ_BANK + i % 2, :]).then_inc(summed, 1)
                else:
                    V.wait_ge(summed, i)
                    V.tensor_tensor(norm[:], norm[:], ps[:, SQ_BANK + i % 2, :], ALU.add).then_inc(summed, 1)

            def rms(j, gi):
                V.wait_ge(rms_base, j + 1)
                V.reciprocal(norm[:], norm[:]).then_inc(rms_ready, 1)
                V.wait_ge(rms_ready, j + 1)
                for k in range(KD + 1):
                    i = j * KD + k
                    if k < KD:
                        if k >= 2:
                            V.wait_ge(h_lo_ready, i - 1)
                        V.scalar_tensor_tensor(out=ps[:, H32_BANK + i % 2, :], in0=xs[:, k, :],
                                               scalar=gains[:, gi, k:k + 1], in1=norm[:],
                                               op0=ALU.mult, op1=ALU.mult).then_inc(h32_ready, 1)
                    if k >= 1:
                        V.wait_ge(h_hi_ready, i)
                        lo_of(h_lo[:, k - 1, :], ps[:, H32_BANK + (i - 1) % 2, :], h_hi[:, k - 1, :]).then_inc(h_lo_ready, 1)

            V.wait_ge(small_in, 16 * N_SMALL)
            V.memset(eps[:], EPS)
            V.tensor_scalar(bg[:], bg[:], 0.5, None, ALU.mult)
            V.tensor_scalar(nsink[:], sink[:], -1.0, None, ALU.mult).then_inc(consts, 1)
            V.wait_ge(consts, 5)
            V.scalar_tensor_tensor(out=alibi[:], in0=alibi[:], scalar=-1.0, in1=alibi[:], op0=ALU.mult,
                                   op1=ALU.max).then_inc(consts, 1)
            V.wait_ge(consts, 6)
            V.wait_ge(far_hi_ready, 1)
            lo_of(far_lo[:], far[:], far_hi[:]).then_inc(far_hi_ready, 1)
            split_lo(0)
            split_lo(1)
            for k in range(KD):
                sum_squares(k, k)
            for layer in range(DEPTH):
                n0 = MIX_START[layer]
                norm_i = 2 * layer
                rms(norm_i, layer)
                for u in range(N_PROJ):
                    n = n0 + u
                    split_lo(n + 2)
                    V.wait_ge(kq_hi_ready, layer * N_PROJ + u + 1)
                    V.scalar_tensor_tensor(out=kq_lo[:, u, :], in0=ps[:, n % 2, :], scalar=SCALE if 4 <= u < 12 else 1.0,
                                           in1=kq_hi[:, u, :].bitcast(F32), op0=ALU.mult,
                                           op1=ALU.subtract).then_inc(drained_dve, 1)
                for u in range(N_V + 1):
                    if u < N_V:
                        split_lo(n0 + U_V + u + 2)
                    if u >= 1:
                        i = layer * N_V + u - 1
                        V.wait_ge(v_hi_ready, i + 1)
                        lo_of(v_lo[:, :, (u - 1) * P:u * P],
                              ps[:, T_BANK + i % 2, :].rearrange("p (t c) -> p t c", c=P),
                              v_hi[:, :, (u - 1) * P:u * P]).then_inc(v_lo_ready, 1)

                def bias_split(hh):
                    if hh < HEADS:
                        H = layer * 2 * HEADS + hh
                        V.wait_ge(bias_hi_ready, H + 1)
                        lo_of(bias_lo[:, H % 2, :], bias[:], bias_hi[:, H % 2, :]).then_inc(bias_lo_ready, 1)

                bias_split(0)
                for tick in range(STEPS + 4):
                    if tick < STEPS:
                        s, st = layer * STEPS + tick, step(tick)
                        c, nk, sc = s % 4, st["nk"], ps[:, S_BANK + s % 2, :]
                        V.wait_ge(scores_ready, s + 1)
                        if st["a"]:
                            V.tensor_reduce(stat[:, 1, c:c + 1], sc[:, 0:nk], AX.X, ALU.max, negate=True).then_inc(nmax_ready, 1)
                        else:
                            V.tensor_reduce(stat[:, 0, c:c + 1], sc[:, 0:nk], AX.X, ALU.max, negate=True).then_inc(max_ready, 1)
                            V.wait_ge(max_ready, layer * STEPS // 2 + tick + 1 - STEPS // 2)
                            V.tensor_tensor(stat[:, 1, c:c + 1], stat[:, 0, c:c + 1],
                                            nsink[:, layer, st["head"]:st["head"] + 1], ALU.min).then_inc(nmax_ready, 1)
                    if 1 <= tick < STEPS + 1:
                        s, st = layer * STEPS + tick - 1, step(tick - 1)
                        c, nk, t = s % 4, st["nk"], probs[:, s % 2, :]
                        V.wait_ge(exp_ready, s + 1)
                        den = stat[:, 2, c:c + 1]
                        if not st["a"]:
                            V.tensor_tensor(stat[:, 4, c:c + 1], den, stat[:, 3, c:c + 1], ALU.add).then_inc(denom, 1)
                            V.wait_ge(denom, layer * STEPS // 2 + tick - STEPS // 2)
                            den = stat[:, 4, c:c + 1]
                        V.reciprocal(stat[:, 5, c:c + 1], den).then_inc(rcp_ready, 1)
                        V.wait_ge(rcp_ready, s + 1)
                        V.tensor_scalar(t[:, 0:nk], t[:, 0:nk], stat[:, 5, c:c + 1], None, ALU.mult).then_inc(probs_ready, 1)
                    if 2 <= tick < STEPS + 2:
                        s, st = layer * STEPS + tick - 2, step(tick - 2)
                        nk = st["nk"]
                        V.wait_ge(pT_hi_ready, s + 1)
                        lo_of(pT_lo[:, s % 2, 0:nk], ps[:, T_BANK + s % 2, 0:nk], pT_hi[:, s % 2, 0:nk]).then_inc(pT_lo_ready, 1)
                    if tick % TT == 1 and tick < STEPS - TT:
                        bias_split(tick // TT + 1)
                    if (tick - 4) in GATES_AT:
                        split_lo(n0 + U_GATE + GATES_AT[tick - 4] + 2)
                    if tick >= 7 and (tick - 7) % 4 == 0:
                        hh = (tick - 7) // 4
                        H = layer * 2 * HEADS + hh
                        st = step(4 * hh)
                        r = st["rows"]
                        V.wait_ge(y_hi_ready, H + 1)
                        lo_of(kq_lo[r:r + HD, st["q"], :], ps[r:r + HD, O_BANK + hh % 2, :],
                              kq_hi[r:r + HD, st["q"], :]).then_inc(y_lo_ready, 1)

                for i in range(N_BR // 2):
                    n = n0 + U_BR + 2 * i
                    split_lo(n + 2)
                    split_lo(n + 3)
                    V.wait_ge(unit_done, n + 2)
                    V.wait_ge(drained_act, N_GATE * (layer + 1))
                    for mm in range(2):
                        m = layer * KD + 2 * i + mm
                        za, zb = branch_banks(i)
                        if m:
                            V.wait_ge(merged_lo, m)
                        V.scalar_tensor_tensor(out=probs[:, 1, :], in0=gates[:, 2 * (2 * i + mm) + 1, :], scalar=1.0,
                                               in1=ps[:, zb + mm, :], op0=ALU.add, op1=ALU.mult)
                        V.scalar_tensor_tensor(out=probs[:, 0, :], in0=gates[:, 2 * (2 * i + mm), :], scalar=1.0,
                                               in1=ps[:, za + mm, :], op0=ALU.add, op1=ALU.mult).then_inc(gated, 1)
                        V.wait_ge(gated, m + 1)
                        V.tensor_tensor(probs[:, 0, :], probs[:, 0, :], probs[:, 1, :], ALU.add).then_inc(merged32, 1)
                        V.wait_ge(merged_hi, m + 1)
                        V.scalar_tensor_tensor(out=h_lo[:, 2 * i + mm, :], in0=probs[:, 0, :], scalar=0.5,
                                               in1=h_hi[:, 2 * i + mm, :].bitcast(F32), op0=ALU.mult,
                                               op1=ALU.subtract).then_inc(merged_lo, 1)
                last = n0 + N_MIX
                for u in range(N_OUT):
                    n = n0 + U_OUT + u
                    if layer == 0 or n + 2 <= last:
                        split_lo(n + 2)
                    V.wait_ge(unit_done, n + 1)
                    V.tensor_tensor(xs[:, u, :], xs[:, u, :], ps[:, T_BANK + n % 2, :], ALU.add).then_inc(x_updated, 1)
                    sum_squares((norm_i + 1) * KD + u, u)
                rms(norm_i + 1, DEPTH + layer)
                if layer == 0:
                    for u in range(N_GU):
                        n = FFN_START + u
                        split_lo(n + 2)
                        f = u // 2
                        if u % 2 == 1:
                            V.wait_ge(silu_ready, f + 1)
                            V.wait_ge(unit_done, n + 1)
                            if f >= 2:
                                V.wait_ge(a_lo_ready, f - 1)
                            V.tensor_tensor(act[:, f % 2, :], silu[:, f % 2, :], ps[:, n % 2, :], ALU.mult).then_inc(act_ready, 1)
                            V.wait_ge(a_hi_ready, f + 1)
                            lo_of(a_lo[:, f, :], act[:, f % 2, :], a_hi[:, f, :]).then_inc(a_lo_ready, 1)
                    for u in range(N_DOWN):
                        n = FFN_START + N_GU + u
                        if (u + 2) % 3 == 2 and u + 2 < N_DOWN:
                            split_lo(n + 2, DOWN_TILES[2] * P)
                        else:
                            split_lo(n + 2)
                        if u % 3 == 2:
                            m = u // 3
                            V.wait_ge(unit_done, n + 1)
                            V.tensor_tensor(xs[:, m, :], xs[:, m, :], ps[:, m % 2, :], ALU.add).then_inc(x_updated, 1)
                            sum_squares(2 * KD + m, m)

            V.sem_inc(m_act_ready, SLOTS)
            V.sem_inc(at_lo_ready, SLOTS)
            steps = [0]

            def link(ins):
                steps[0] += 1
                ins.then_inc(route_step, 1)
                V.wait_ge(route_step, steps[0])

            def each(a):
                return a.unsqueeze(2).to_broadcast([P, TT, EXPERTS])

            V.wait_ge(rinv_turned, 1)
            link(V.tensor_copy(r1[:, 7, :], ps[:, 7, :].rearrange("p (t c) -> p t c", c=P)[:, :, 0]))
            V.wait_ge(route_consts, 1)
            rank8, twice_e, lg, hit, key, first_, rest, second, posn, step_, dest = (rt[:, j, :, :] for j in range(11))
            V.wait_ge(logits_turned, 1)
            link(V.tensor_copy(lg, ps[:, 2, :].rearrange("p (t c) -> p t c", c=P)[:, :, 0:EXPERTS]))

            def largest(values, chosen, top):
                link(V.tensor_reduce(top, values, AX.X, ALU.max))
                link(V.tensor_tensor(hit, values, each(top), ALU.is_equal))
                link(V.tensor_tensor(key, hit, rank8, ALU.mult))
                link(V.tensor_reduce(r1[:, 6, :], key, AX.X, ALU.max))
                link(V.tensor_tensor(chosen, key, each(r1[:, 6, :]), ALU.is_equal))

            largest(lg, first_, r1[:, 0, :])
            link(V.scalar_tensor_tensor(out=rest, in0=first_, scalar=-3.0e38, in1=lg, op0=ALU.mult, op1=ALU.add))
            largest(rest, second, r1[:, 1, :])
            V.tensor_tensor(picks[:], first_, second, ALU.add).then_inc(picks_ready, 1)
            V.tensor_tensor(r1[:, 2, :], r1[:, 1, :], r1[:, 0, :], ALU.subtract).then_inc(gap_ready, 1)
            V.wait_ge(ranks_ready, 1)
            link(V.tensor_copy(posn, ps[:, 3, 0:TT * EXPERTS].rearrange("p (t e) -> p t e", e=EXPERTS)))
            link(V.scalar_tensor_tensor(out=dest, in0=posn, scalar=float(LISTS), in1=twice_e, op0=ALU.mult, op1=ALU.add))
            for edge, add in ((P, 1), (2 * P, SLOTS * EXPERTS - 1), (3 * P, 1)):
                link(V.tensor_scalar(step_, posn, float(edge), float(add - LISTS * P), ALU.is_ge, ALU.mult))
                link(V.tensor_tensor(dest, dest, step_, ALU.add))
            for c, chosen in enumerate((first_, second)):
                link(V.tensor_tensor(key, dest, chosen, ALU.mult))
                link(V.tensor_reduce(r1[:, 10 + c, :], key, AX.X, ALU.add))
                link(V.tensor_copy(place[:, :, c], r1[:, 10 + c, :]))
            link(V.tensor_copy(counts[:], ps[:, 3, 64:64 + EXPERTS]))
            V.tensor_reduce(most[:], ps[:, 3, 64:64 + EXPERTS], AX.X, ALU.max).then_inc(places_ready, 1)
            V.wait_ge(places_ready, 1)
            V.sem_inc(counts_ready, 1)
            V.wait_ge(gap_exp, 1)
            link(V.tensor_scalar(r1[:, 2, :], r1[:, 3, :], 1.0, None, ALU.add))
            link(V.reciprocal(r1[:, 4, :], r1[:, 2, :]))
            link(V.tensor_tensor(r1[:, 5, :], r1[:, 4, :], r1[:, 3, :], ALU.mult))
            V.wait_ge(rows_in, 16)
            V.wait_ge(route_consts, 2)
            for t in range(TT):
                V.wait_ge(x_copied, t + 1)
                if t >= 2:
                    V.wait_ge(h_row_sent[t % 2], 16 * (2 if t % 2 == 0 else 1))
                V.scalar_tensor_tensor(out=h_rows[:, t % 2, :], in0=x_rows[:, t, :], scalar=r1[:, 7, t:t + 1], in1=g_row[:],
                                       op0=ALU.mult, op1=ALU.mult).then_inc(h_row_ready, 1)

            def expert_lo(done, u):
                cols = UNITS[u % M_UNITS][3]
                V.wait_ge(m_hi_ready, done + (u + 1))
                V.tensor_tensor(m_lo[:, u % M_SPL, 0:cols], m_raw[:, u % M_RAW, 0:cols],
                                m_hi[:, u % M_SPL, 0:cols].bitcast(F32), ALU.subtract).then_inc(m_lo_ready, 1)

            def turned_x(done, sl):
                for hb in range(2):
                    k = slice(4 * hb, 4 * hb + 4)
                    V.wait_ge(xt_hi_ready, done + (2 * sl + hb + 1))
                    lo_of(xt_lo[:, k, sl, :], ps[:, hb, :].rearrange("p (k c) -> p k c", c=P),
                          xt_hi[:, k, sl, :]).then_inc(xt_lo_ready, 1)

            for u in range(M_SPL):
                expert_lo(0, u)
            turned_x(0, 0)
            turned_x(0, 1)

            def passes(first):
                with V.Fori(0, N_SEC) as i:
                    for u in range(M_UNITS):
                        for c in range(len(CHUNKS)):
                            if u == CHUNK_END[c]["up"]:
                                w = CHUNKS[c] * P
                                V.wait_ge(m_done, i * M_UNITS + (first * M_UNITS + u + 1))
                                for sl in range(SLOTS):
                                    V.wait_ge(m_silu_ready, i * 6 + (6 * first + SLOTS + 2 * c + sl + 1))
                                    V.wait_ge(at_turned, i * 6 + (6 * first + 2 * c + sl + 1))
                                    V.tensor_tensor(m_act[:, sl, 0:w], m_silu[:, sl, 0:w], ps[:, 2 + sl, 0:w],
                                                    ALU.mult).then_inc(m_act_ready, 1)
                        expert_lo(i * M_UNITS + first * M_UNITS, u + M_SPL)
                        if u in TURNED_AT:
                            c = TURNED_AT[u]
                            nb = CHUNKS[c]
                            for sl in range(SLOTS):
                                V.wait_ge(at_hi_ready, i * 6 + (6 * first + 2 * c + sl + 1))
                                lo_of(at_lo[:, 4 * c:4 * c + nb, sl, :], ps[:, 4 + sl, 0:nb * P].rearrange("p (k c) -> p k c", c=P),
                                      at_hi[:, 4 * c:4 * c + nb, sl, :]).then_inc(at_lo_ready, 1)
                        if u in TURN_X:
                            turned_x(i * 4 + 4 * (first + 1), TURN_X.index(u))

            passes(0)
            with V.If(V.value_load(most[0:1, 0:1], min_val=0, max_val=T) > CAP):
                passes(N_SEC)
            V.wait_ge(rows_in, 32)
            for t in range(TT + 1):
                if t < TT:
                    V.wait_ge(y_back[t % 2], 16 * (t // 2 + 1))
                    V.scalar_tensor_tensor(out=x_rows[:, t, :], in0=y_in[:, t % 2, 0, :], scalar=r1[:, 4, t:t + 1],
                                           in1=x_rows[:, t, :], op0=ALU.mult, op1=ALU.add).then_inc(mix_step, 1)
                    V.wait_ge(mix_step, t + 1)
                    V.scalar_tensor_tensor(out=x_rows[:, t, :], in0=y_in[:, t % 2, 1, :], scalar=r1[:, 5, t:t + 1],
                                           in1=x_rows[:, t, :], op0=ALU.mult, op1=ALU.add).then_inc(mixed, 1)
                if t >= 1:
                    V.wait_ge(root_ready, t)
                    V.reciprocal(r1[:, 6, t - 1:t], r1[:, 9, t - 1:t]).then_inc(inv_ready, 1)
                    V.wait_ge(inv_ready, t)
                    V.scalar_tensor_tensor(out=x_rows[:, t - 1, :], in0=x_rows[:, t - 1, :], scalar=r1[:, 6, t - 1:t],
                                           in1=gf_row, op0=ALU.mult, op1=ALU.mult).then_inc(out_ready, 1)

        @block.tensor
        def _(E):
            def unit_ready(n):
                E.wait_ge(lo_ready, n + 1)

            def tile_products(n, i, bank, hi, lo, first, final):
                wh, wl = w_hi[:, n % SPL, i * P:(i + 1) * P], w_lo[:, n % SPL, i * P:(i + 1) * P]
                E.matmul(ps[:, bank, :], wh, hi, start=first, stop=False)
                E.matmul(ps[:, bank, :], wh, lo, start=False, stop=False)
                return E.matmul(ps[:, bank, :], wl, hi, start=False, stop=final)

            def mean_square(j):
                E.wait_ge(summed, (j + 1) * KD)
                E.matmul(ps[:, SUM_BANK, :], ones[:], norm[:], start=True, stop=True).then_inc(sum_bcast, 1)

            def x_unit(n, bank, k0=0, k1=KD, first_of=None):
                unit_ready(n)
                for k in range(k0, k1):
                    mm = tile_products(n, k, bank, h_hi[:, k, :], h_lo[:, k, :], k == 0, k == KD - 1)
                return mm

            def turn_v(layer, u):
                i = layer * N_V + u
                E.wait_ge(vT_copied, i + 1)
                if i >= 2:
                    E.wait_ge(v_lo_ready, i - 1)
                for t in range(TT):
                    tr = E.transpose(ps[:, T_BANK + i % 2, t * P:(t + 1) * P], probs[:, i % 2, t * P:(t + 1) * P], ident[:])
                tr.then_inc(vT_turned, 1)

            E.wait_ge(consts, 6)
            E.wait_ge(flip_ready, 1)
            E.wait_ge(far_hi_ready, 2)
            mean_square(0)
            for layer in range(DEPTH):
                n0 = MIX_START[layer]
                norm_i = 2 * layer
                dve0 = layer * N_PROJ
                for u in range(N_PROJ):
                    n = n0 + u
                    if u >= 2:
                        E.wait_ge(drained_dve, dve0 + u - 1)
                    unit_ready(n)
                    for k in range(KD):
                        if u == 0:
                            E.wait_ge(h_lo_ready, norm_i * KD + k + 1)
                        mm = tile_products(n, k, n % 2, h_hi[:, k, :], h_lo[:, k, :], k == 0, k == KD - 1)
                    mm.then_inc(unit_done, 1)
                for u in range(N_V + 1):
                    n = n0 + U_V + u
                    if u < N_V:
                        if u < 2:
                            E.wait_ge(drained_dve, dve0 + N_PROJ - 1 + u)
                        else:
                            E.wait_ge(vT_copied, layer * N_V + u - 1)
                        x_unit(n, n % 2).then_inc(unit_done, 1)
                    if u >= 1:
                        turn_v(layer, u - 1)
                E.wait_ge(v_lo_ready, layer * N_V + N_V)
                E.wait_ge(drained_dve, dve0 + N_PROJ)

                for tick in range(STEPS + 3):
                    def gate_part(half):
                        g = tick // 4
                        n = n0 + U_GATE + g
                        if tick % 4 == 0 and half == 0:
                            unit_ready(n)
                            if g < 2:
                                E.wait_ge(vT_copied, layer * N_V + N_V - 1 + g)
                            else:
                                E.wait_ge(drained_act, layer * N_GATE + g - 1)
                        k = 2 * (tick % 4) + half
                        mm = tile_products(n, k, n % 2, h_hi[:, k, :], h_lo[:, k, :], k == 0, k == KD - 1)
                        if k == KD - 1:
                            mm.then_inc(unit_done, 1)

                    if 2 <= tick < STEPS + 2:
                        s, st = layer * STEPS + tick - 2, step(tick - 2)
                        E.wait_ge(probs_ready, s + 1)
                        if s >= 2:
                            E.wait_ge(pT_lo_ready, s - 1)
                        for b in range(st["nk"] // P):
                            tr = E.transpose(ps[:, T_BANK + s % 2, b * P:(b + 1) * P], probs[:, s % 2, b * P:(b + 1) * P], ident[:])
                        tr.then_inc(pT_ready, 1)
                    if tick < STEPS:
                        s, st = layer * STEPS + tick, step(tick)
                        r, k0, nk, qb = st["rows"], st["k0"], st["nk"], st["qb"]
                        H = layer * 2 * HEADS + st["hh"]
                        if s >= 2:
                            E.wait_ge(exp_ready, s - 1)
                        near = min(nk, 2 * P)
                        out = ps[:, S_BANK + s % 2, 0:nk]
                        E.wait_ge(bias_hi_ready, H + 1)
                        E.matmul(out[:, nk - near:nk], flip_r[:], bias_hi[:, H % 2, 2 * P - near:2 * P], start=True, stop=False)
                        if st["a"]:
                            E.wait_ge(bias_lo_ready, layer * HEADS + st["hh"] + 1)
                            E.matmul(out[:, nk - near:nk], flip_r[:], bias_lo[:, H % 2, 2 * P - near:2 * P], start=False, stop=False)
                            if nk > near:
                                for part in (far_hi, far_lo):
                                    E.matmul(out[:, 0:nk - near], flip_r[:],
                                             part[:, layer, st["hh"]:st["hh"] + 1].to_broadcast([P, nk - near]), start=False, stop=False)
                        q_hi = kq_hi[r:r + HD, st["q"], qb * P:(qb + 1) * P]
                        q_lo = kq_lo[r:r + HD, st["q"], qb * P:(qb + 1) * P]
                        k_hi = kq_hi[r:r + HD, st["k"], k0:k0 + nk]
                        k_lo = kq_lo[r:r + HD, st["k"], k0:k0 + nk]
                        E.matmul(out, q_hi, k_hi, start=False, stop=False)
                        E.matmul(out, q_hi, k_lo, start=False, stop=False)
                        E.matmul(out, q_lo, k_hi, start=False, stop=True).then_inc(scores_ready, 1)
                        gate_part(0)
                    if 3 <= tick:
                        s, st = layer * STEPS + tick - 3, step(tick - 3)
                        hh, qb, nb = st["hh"], st["qb"], st["nk"] // P
                        E.wait_ge(pT_lo_ready, s + 1)
                        if qb == 0 and hh >= 2:
                            E.wait_ge(y_lo_ready, layer * 2 * HEADS + hh - 1)
                        out = ps[:, O_BANK + hh % 2, qb * P:(qb + 1) * P]
                        for b in range(nb):
                            kt, vc = st["k0"] // P + b, slice(st["v"] * P, (st["v"] + 1) * P)
                            p_hi, p_lo = pT_hi[:, s % 2, b * P:(b + 1) * P], pT_lo[:, s % 2, b * P:(b + 1) * P]
                            E.matmul(out, v_hi[:, kt, vc], p_hi, start=b == 0, stop=False)
                            E.matmul(out, v_hi[:, kt, vc], p_lo, start=False, stop=False)
                            mm = E.matmul(out, v_lo[:, kt, vc], p_hi, start=False, stop=b == nb - 1)
                        mm.then_inc(pv_done, 1)
                    if tick < STEPS:
                        gate_part(1)

                E.wait_ge(y_lo_ready, (layer + 1) * 2 * HEADS)
                E.wait_ge(drained_act, (layer + 1) * N_GATE)
                for i in range(N_BR // 2):
                    if i >= 2:
                        E.wait_ge(merged_lo, layer * KD + 2 * (i - 1))
                    for which, bank in enumerate(branch_banks(i)):
                        n = n0 + U_BR + 2 * i + which
                        unit_ready(n)
                        for mm_ in range(2):
                            for k in range(4):
                                y = 4 + 4 * which + k
                                mm = tile_products(n, 4 * mm_ + k, bank + mm_, kq_hi[:, y, :], kq_lo[:, y, :], k == 0, k == 3)
                        mm.then_inc(unit_done, 1)
                for u in range(N_OUT):
                    n = n0 + U_OUT + u
                    unit_ready(n)
                    if u >= 2:
                        E.wait_ge(x_updated, 2 * layer * KD + u - 1)
                    if u == 0:
                        E.wait_ge(merged_lo, layer * KD + KD - 2)
                    for k in range(KD):
                        if u == 0 and k >= KD - 2:
                            E.wait_ge(merged_lo, layer * KD + k + 1)
                        mm = tile_products(n, k, T_BANK + n % 2, h_hi[:, k, :], h_lo[:, k, :], k == 0, k == KD - 1)
                    mm.then_inc(unit_done, 1)
                mean_square(norm_i + 1)
                if layer == 0:
                    E.wait_ge(x_updated, KD)
                    for u in range(N_GU):
                        n = FFN_START + u
                        unit_ready(n)
                        f = u // 2
                        if f >= 1:
                            if u % 2 == 0:
                                E.wait_ge(silu_ready, f)
                            else:
                                E.wait_ge(act_ready, f)
                        for k in range(KD):
                            if u == 0:
                                E.wait_ge(h_lo_ready, KD + k + 1)
                            mm = tile_products(n, k, n % 2, h_hi[:, k, :], h_lo[:, k, :], k == 0, k == KD - 1)
                        mm.then_inc(unit_done, 1)
                    E.wait_ge(act_ready, KF)
                    for u in range(N_DOWN):
                        n = FFN_START + N_GU + u
                        m, part = u // 3, u % 3
                        unit_ready(n)
                        if part == 0 and m >= 2:
                            E.wait_ge(x_updated, KD + m - 1)
                        for t in range(DOWN_TILES[part]):
                            f = 8 * part + t
                            if m == 0:
                                E.wait_ge(a_lo_ready, f + 1)
                            mm = tile_products(n, t, m % 2, a_hi[:, f, :], a_lo[:, f, :], f == 0, f == KF - 1)
                        mm.then_inc(unit_done, 1)
                    mean_square(2)

            def turn_x(t):
                if t:
                    E.wait_ge(x_copied, t)
                for k in range(KD):
                    tr = E.transpose(ps[:, k // 4, (k % 4) * P:(k % 4 + 1) * P], xs[:, k, t * P:(t + 1) * P], ident[:])
                tr.then_inc(x_turned, 1)

            E.sem_inc(at_turned, SLOTS)
            turn_x(0)
            E.wait_ge(rms_ready, 4)
            for t in range(TT):
                tr = E.transpose(ps[:, 7, t * P:(t + 1) * P], norm[:, t * P:(t + 1) * P], ident[:])
            tr.then_inc(rinv_turned, 1)
            unit_ready(U_ROUTER)
            for k in range(KD):
                E.wait_ge(h_lo_ready, 3 * KD + k + 1)
                mm = tile_products(U_ROUTER, k, 6, h_hi[:, k, :], h_lo[:, k, :], k == 0, k == KD - 1)
            mm.then_inc(unit_done, 1)
            E.wait_ge(logits_ready, 1)
            for t in range(TT):
                tr = E.transpose(ps[:, 2, t * P:(t + 1) * P], logits_T[:, t * P:(t + 1) * P], ident[:])
            tr.then_inc(logits_turned, 1)
            for t in range(1, TT):
                turn_x(t)
            E.wait_ge(picks_ready, 1)
            for t in range(TT):
                for b in range(t + 1):
                    E.matmul(ps[:, 3, t * EXPERTS:(t + 1) * EXPERTS], before[:] if b == t else all_ones[:], picks[:, b, :],
                             start=b == 0, stop=b == t)
            for b in range(TT):
                mm = E.matmul(ps[:, 3, 64:64 + EXPERTS], all_ones[:], picks[:, b, :], start=b == 0, stop=b == TT - 1)
            mm.then_inc(ranks_ready, 1)
            E.wait_ge(counts_ready, 1)
            E.wait_ge(x_copied, TT)
            E.wait_ge(rinv_turned, 1)

            def turn_rows(done, sl, p16):
                E.wait_ge(xg_in[sl], p16)
                for k in range(KD):
                    if sl and k % 4 == 0:
                        E.wait_ge(xt_lo_ready, done + (k // 4 + 1))
                    tr = E.transpose(ps[:, k // 4, (k % 4) * P:(k % 4 + 1) * P], xg[:, sl, k * P:(k + 1) * P], ident[:])
                    if k % 4 == 3:
                        tr.then_inc(xt_turned, 1)

            turn_rows(0, 0, 16)
            turn_rows(0, 1, 16)

            def passes(first, always_both):
                with E.Fori(0, N_SEC) as i:
                    def pass_of(slots):
                        def three(out, a_hi_, a_lo_, u, lo_col, n, start, stop):
                            wh, wl = m_hi[:, u % M_SPL, lo_col:lo_col + n], m_lo[:, u % M_SPL, lo_col:lo_col + n]
                            E.matmul(out, a_hi_, wh, start=start, stop=False)
                            E.matmul(out, a_hi_, wl, start=False, stop=False)
                            return E.matmul(out, a_lo_, wh, start=False, stop=stop)

                        def turn_act(c):
                            for sl in range(SLOTS):
                                E.wait_ge(m_act_ready, i * 6 + (6 * first + SLOTS + 2 * c + sl + 1))
                                E.wait_ge(at_lo_ready, i * 6 + (6 * first + 2 * c + sl + 1))
                                if sl < slots:
                                    for b in range(CHUNKS[c]):
                                        tr = E.transpose(ps[:, 4 + sl, b * P:(b + 1) * P], m_act[:, sl, b * P:(b + 1) * P], ident[:])
                                    tr.then_inc(at_turned, 1)
                                else:
                                    E.wait_ge(at_turned, i * 6 + (6 * first + SLOTS + 2 * c + sl))
                                    E.sem_inc(at_turned, 1)

                        E.wait_ge(xt_lo_ready, i * 4 + (4 * first + 4))
                        for u, (what, c, j, cols) in enumerate(UNITS):
                            w = cols // 2
                            E.wait_ge(m_lo_ready, i * M_UNITS + (first * M_UNITS + u + 1))
                            if what != "down":
                                if j == 0 and c:
                                    E.wait_ge(m_silu_ready if what == "gate" else m_act_ready, i * 6 + (6 * first + SLOTS + 2 * c))
                                if j == 0 and not c and what == "up":
                                    E.wait_ge(y_copied, i * SLOTS + (SLOTS * first + SLOTS))
                                for sl in range(slots):
                                    for k in (2 * j, 2 * j + 1):
                                        mm = three(ps[:, (0 if what == "gate" else 2) + sl, 0:w], xt_hi[:, k, sl, :],
                                                   xt_lo[:, k, sl, :], u, (k % 2) * w, w, k == 0, k == KD - 1)
                                mm.then_inc(m_done, 1)
                                if c and what == "gate" and j == 0:
                                    turn_act(c - 1)
                            else:
                                f = j
                                for sl in range(slots):
                                    if f == 0 and sl:
                                        E.wait_ge(m_act_ready, i * 6 + (6 * first + SLOTS + 2 * len(CHUNKS)))
                                    if f % 4 == 0:
                                        E.wait_ge(at_lo_ready, i * 6 + (6 * first + SLOTS + 2 * (f // 4) + sl + 1))
                                    for half in range(2):
                                        mm = three(ps[:, Y_BANKS[sl] + half, :], at_hi[:, f, sl, :], at_lo[:, f, sl, :], u,
                                                   half * T, T, f == 0, f == KFE - 1)
                                mm.then_inc(m_done, 1)
                                if u == TURN_LAST:
                                    turn_act(2)
                                if u in TURN_X:
                                    if u == TURN_X[0]:
                                        E.wait_ge(m_silu_ready, i * 6 + (6 * first + SLOTS + 2 * len(CHUNKS)))
                                    turn_rows(i * 4 + 4 * (first + 1), TURN_X.index(u), i * 16 + 16 * (first + 2))

                    if always_both:
                        pass_of(SLOTS)
                    else:
                        with E.If(E.value_load(counts[0:1, bass.ds(i, 1)], min_val=0, max_val=T) > P):
                            pass_of(SLOTS)
                        with E.Else():
                            pass_of(1)

            passes(0, False)
            with E.If(E.value_load(most[0:1, 0:1], min_val=0, max_val=T) > CAP):
                passes(N_SEC, True)


def host_layout(i):
    import numpy as np
    f = lambda a: np.ascontiguousarray(a)
    x = np.asarray(i["x"])[0]
    A, Bw = 512, 512
    w_in = np.asarray(i["w_in"])
    o = np.cumsum([0, 512, 512, 512, 512, 128, 128, 2048])
    cols = lambda a, n: np.arange(a, a + n)
    cb = np.concatenate([cols(64 * (j + 4 * g), 64) for j in range(4) for g in range(2)])
    gate_cols = np.concatenate([cols(o[6] + g * 1024 + m * 128, 128) for m in range(8) for g in range(2)])
    order = np.concatenate([cols(o[1], 512), cols(o[0], 512), o[3] + cb, cols(o[4], 128), cols(o[2], 512), cols(o[5], 128), gate_cols])
    units = lambda w, k, per: w.reshape(k, 128, -1, per, 128).transpose(2, 1, 3, 0, 4).reshape(-1, 128, per * k * 128)
    both = lambda fn, w: f(np.stack([fn(np.asarray(w)[l]) for l in range(2)]))
    rb = np.asarray(i["rel_bias"])
    rev = rb[:, :, ::-1][:, :, :256]
    ext = np.concatenate([np.repeat(rev[:, :, :1], 127, axis=2), rev, rev[:, :, -1:]], axis=2)
    pk = lambda g: np.asarray(g).reshape(-1, 8, 128).transpose(2, 0, 1)
    bgt = np.asarray(i["b_gate"]).reshape(2, 2, 8, 128).transpose(3, 0, 2, 1).reshape(128, 2, 16)
    gu = np.stack([np.asarray(i["ffn_w_gate"])[0].reshape(1024, 22, 128), np.asarray(i["ffn_w_up"])[0].reshape(1024, 22, 128)], axis=2).reshape(1024, -1)
    dn = np.asarray(i["ffn_w_down"])[0]
    wr = np.zeros((1024, 128), np.float32)
    wr[:, :8] = np.asarray(i["w_router"])[0]
    wr = wr.reshape(8, 128, 128).transpose(1, 0, 2).reshape(128, 1024)
    def chunk(w, a, n):
        return w[:, :, a:a + n].reshape(8, 4, 2, 128, n).transpose(0, 1, 3, 2, 4).reshape(8, 4, 128, 2 * n)
    g, u = np.asarray(i["moe_w_gate"])[0], np.asarray(i["moe_w_up"])[0]
    mgu = (np.stack([np.concatenate([chunk(g, a, 512), chunk(u, a, 512)], axis=1) for a in (0, 512)]),
           np.concatenate([chunk(g, 1024, 384), chunk(u, 1024, 384)], axis=1))
    return dict(
        xT=f(x.T.reshape(8, 128, 512).transpose(1, 0, 2)),
        g_mix=f(pk(i["norm_mix"])), w_in=both(lambda w: units(w[:, order], 8, 1), w_in), b_gate=f(bgt),
        rel_ext=f(ext), sinks=f(np.asarray(i["sinks"])),
        w_a=both(lambda w: units(w, 4, 2), i["w_branch_a"]),
        w_b=both(lambda w: units(w[cb], 4, 2), i["w_branch_b"]),
        w_out=both(lambda w: units(w, 8, 1), i["w_out"]),
        g_ffn=f(pk(i["norm_ffn"])), w_gu=f(units(gu, 8, 1)), w_down=f(units(dn, 22, 1)),
        w_router=f(wr), moe_g01=f(mgu[0]), moe_g2=f(mgu[1]),
        moe_down=f(np.asarray(i["moe_w_down"])[0].reshape(8, 11, 128, 1024)),
        g_ffn_row=f(np.asarray(i["norm_ffn"])[1:2]), g_final_row=f(np.asarray(i["norm_final"])[None]),
    )


_OUT = (T, D)


def kernel(**inputs):
    import concourse.bacc as _bacc
    import numpy as _np
    from concourse import mybir as _mybir
    from concourse.bass_utils import run_bass_kernel_spmd as _run

    nc = _bacc.Bacc("TRN2", target_bir_lowering=False, num_devices=1)
    arrays = host_layout(inputs)
    ap = {n: nc.dram_tensor(n, a.shape, _mybir.dt.from_np(a.dtype), kind="ExternalInput").ap() for n, a in arrays.items()}
    out = nc.dram_tensor("out", _OUT, F32, kind="ExternalOutput").ap()
    moe_gu = (ap.pop("moe_g01"), ap.pop("moe_g2"))
    build_kernel(nc, moe_gu=(moe_gu[0][0], moe_gu[0][1], moe_gu[1]), out=out, **ap)
    r = _run(nc, [arrays], core_ids=[0])
    return _np.asarray(r.results[0]["out"]).reshape(1, *_OUT)
```

```python
from contextlib import ExitStack

import concourse.bass as bass
from concourse import mybir

F32 = mybir.dt.float32
F32R = mybir.dt.float32r
BF16 = mybir.dt.bfloat16
U32 = mybir.dt.uint32
I32 = mybir.dt.int32
ALU = mybir.AluOpType
ACT = mybir.ActivationFunctionType
AX = mybir.AxisListType

P = 128
D = 1024
T = 512
DEPTH = 2
KD = D // P
TT = T // P
HEADS = 8
HD = 64
D_FF = 2816
KF = D_FF // P
EPS = 1e-6
SCALE = HD ** -0.5
MASKED = -1e30

UNIT = 8 * P
RAW = 4
SPL = 2

N_PROJ, N_V, N_GATE, N_BR, N_OUT = 13, 5, 16, 8, 8
U_V = N_PROJ
U_GATE = U_V + N_V
U_BR = U_GATE + N_GATE
U_OUT = U_BR + N_BR
N_MIX = U_OUT + N_OUT
N_GU = 2 * KF
DOWN_TILES = (8, 8, 6)
N_DOWN = 3 * KD
N_FFN = N_GU + N_DOWN
MIX_START = (0, N_MIX + N_FFN)
FFN_START = N_MIX
STEPS = 2 * HEADS * TT
PT_BLOCKS = 10

U_ROUTER = MIX_START[1] + N_MIX
EXPERTS = 8
D_FFE = 1408
KFE = D_FFE // P
CHUNKS = (4, 4, 3)
M_RAW, M_SPL = 7, 5
M_UNITS = 8 * len(CHUNKS) + KFE
SLOTS = 2
CAP = SLOTS * P
HALVES = T // CAP
LISTS = HALVES * EXPERTS * SLOTS
PAD_H, PAD_Y = T, 2 * T


def build_kernel(nc, xT, g_mix, w_in, b_gate, rel_ext, sinks, w_a, w_b, w_out, g_ffn, w_gu, w_down, w_router,
                 moe_gu, moe_down, g_ffn_row, g_final_row, out):
    ctx = ExitStack()
    with ctx:
        def sb(name, shape, dt=F32, where=ctx):
            return where.enter_context(nc.sbuf_tensor(name, shape, dt))

        def sem(name):
            return ctx.enter_context(nc.semaphore(name))

        norm = sb("norm", [P, T])
        ident = sb("ident", [P, P])
        ones = sb("ones", [P, P])
        mean_of = sb("mean_of", [P, 1])
        warm = sb("warm", [P, 1])
        idle = sb("idle", [P, P], BF16)
        eps = sb("eps", [P, 1])
        root_ = sb("root_", [P, TT])
        rinv = sb("rinv", [P, 2 * DEPTH, TT])
        gains = sb("gains", [P, 2 * DEPTH, KD])

        dense = ExitStack()
        xs = sb("xs", [P, KD, T], F32, dense)
        h_hi = sb("h_hi", [P, KD, T], F32R, dense)
        h_lo = sb("h_lo", [P, KD, T], F32R, dense)
        raw = sb("raw", [P, RAW, UNIT], F32, dense)
        w_hi = sb("w_hi", [P, SPL, UNIT], F32R, dense)
        w_lo = sb("w_lo", [P, SPL, UNIT], F32R, dense)

        attn = ExitStack()
        gates = sb("gates", [P, N_GATE, T], F32, attn)
        kq_hi = sb("kq_hi", [P, N_PROJ, T], F32R, attn)
        kq_lo = sb("kq_lo", [P, N_PROJ, T], F32R, attn)
        v_hi = sb("v_hi", [P, TT, N_V * P], F32R, attn)
        v_lo = sb("v_lo", [P, TT, N_V * P], F32R, attn)
        probs = sb("probs", [P, 2, T], F32, attn)
        pT_hi = sb("pT_hi", [P, PT_BLOCKS, P], F32R, attn)
        pT_lo = sb("pT_lo", [P, PT_BLOCKS, P], F32R, attn)
        bias = norm[:, 0:2 * P]
        bias_hi = sb("bias_hi", [P, 2, 2 * P], F32R, attn)
        bias_lo = sb("bias_lo", [P, 2, 2 * P], F32R, attn)
        flip = probs[:, 0, 0:P]
        flip_r = sb("flip_r", [P, P], F32R, attn)
        alibi = sb("alibi", [P, 2 * P], F32, attn)
        far = sb("far", [P, DEPTH, HEADS], F32, attn)
        sink = sb("sink", [P, DEPTH, HEADS], F32, attn)
        nsink = sb("nsink", [P, DEPTH, HEADS], F32, attn)
        nfar = sb("nfar", [P, DEPTH, HEADS], F32, attn)
        bg = sb("bg", [P, DEPTH, N_GATE], F32, attn)
        stat = sb("stat", [P, 6, 4], F32, attn)
        attn.close()

        ffn = ExitStack()
        a_hi = sb("a_hi", [P, KF, T], F32R, ffn)
        a_lo = sb("a_lo", [P, KF, T], F32R, ffn)
        silu = sb("silu", [P, 2, T], F32, ffn)
        act = sb("act", [P, 2, T], F32, ffn)
        ffn.close()

        routed = ExitStack()
        m_raw = sb("m_raw", [P, M_RAW, UNIT], F32, routed)
        m_hi = sb("m_hi", [P, M_SPL, UNIT], F32R, routed)
        m_lo = sb("m_lo", [P, M_SPL, UNIT], F32R, routed)
        x_rows = sb("x_rows", [P, TT, D], F32, routed)
        h_rows = sb("h_rows", [P, TT, D], F32, routed)
        g_row = sb("g_row", [P, D], F32, routed)
        rt = sb("rt", [P, 14, TT, EXPERTS], F32, routed)
        r1 = sb("r1", [P, 12, TT], F32, routed)
        picks = sb("picks", [P, TT, EXPERTS], BF16, routed)
        before = sb("before", [P, P], BF16, routed)
        all_ones = sb("all_ones", [P, P], BF16, routed)
        spot = sb("spot", [P, 8, 2 * TT], F32, routed)
        entry = sb("entry", [P, 2 * TT, 2], F32, routed)
        zeros = sb("zeros", [1, D], F32, routed)
        numbers = sb("numbers", [P, P], F32, routed)
        in_column = sb("in_column", [P, 2 * TT, LISTS], F32, routed)
        row_hit = sb("row_hit", [P, 2 * TT, P], F32R, routed)
        entry_hit = sb("entry_hit", [P, 2 * TT, LISTS, 2], F32R, routed)
        lists = sb("lists", [P, LISTS, 2], U32, routed)
        counts = sb("counts", [P, EXPERTS], I32, routed)
        most = sb("most", [P, 1], I32, routed)
        routed.close()
        dense.close()

        expert = ExitStack()
        xg = sb("xg", [P, SLOTS, D], F32, expert)
        xt_hi = sb("xt_hi", [P, KD, SLOTS, P], F32R, expert)
        xt_lo = sb("xt_lo", [P, KD, SLOTS, P], F32R, expert)
        m_silu = sb("m_silu", [P, SLOTS, T], F32, expert)
        m_act = sb("m_act", [P, SLOTS, T], F32, expert)
        at_hi = sb("at_hi", [P, KFE, SLOTS, P], F32R, expert)
        at_lo = sb("at_lo", [P, KFE, SLOTS, P], F32R, expert)
        y_stage = sb("y_stage", [P, SLOTS, D], F32, expert)
        y_in = sb("y_in", [P, 2, 2, D], F32, expert)
        expert.close()
        logits_T = y_in[:, 0, 0, 0:T]
        gf_row = g_row[:]

        def y_of(t):
            return y_in[:, t, :, :] if t < 2 else h_rows[:, 2 * (t - 2):2 * (t - 1), :]


        h_dram = nc.dram_tensor("h_dram", [T + 1, D], F32, kind="Internal").ap()
        y_dram = nc.dram_tensor("y_dram", [2 * T, D], F32, kind="Internal").ap()

        ps = ctx.enter_context(nc.psum_tensor("ps", [P, 8, T], F32))
        S_BANK, T_BANK, O_BANK, SUM_BANK = 2, 4, 6, 7
        SQ_BANK, H32_BANK, IDLE_BANK = 2, 4, 6

        raw_full = [sem(f"raw_full{i}") for i in range(RAW)]
        hi_ready, lo_ready = sem("hi_ready"), sem("lo_ready")
        unit_done = sem("unit_done")
        small_in = sem("small_in")
        x_in = [sem(f"x_in{k}") for k in range(KD)]
        basics, consts = sem("basics"), sem("consts")
        const_step = sem("const_step")
        drained_act, drained_dve = sem("drained_act"), sem("drained_dve")
        x_updated, squared, summed = sem("x_updated"), sem("squared"), sem("summed")
        mean_ready, norm_root, rinv_ready, diag_ready, rinv_spread = (sem(n) for n in ("mean_ready", "norm_root", "rinv_ready", "diag_ready", "rinv_spread"))
        h32_ready, h_hi_ready, h_lo_ready = sem("h32_ready"), sem("h_hi_ready"), sem("h_lo_ready")
        kq_hi_ready = sem("kq_hi_ready")
        vT_copied, vT_turned, v_hi_ready, v_lo_ready = sem("vT_copied"), sem("vT_turned"), sem("v_hi_ready"), sem("v_lo_ready")
        bias_in, bias_masked, bias_hi_ready, bias_lo_ready = sem("bias_in"), sem("bias_masked"), sem("bias_hi_ready"), sem("bias_lo_ready")
        flip_ready = sem("flip_ready")
        scores_ready, max_ready, nmax_ready = sem("scores_ready"), sem("max_ready"), sem("nmax_ready")
        sink_exp, exp_ready, denom, rcp_ready, probs_ready = sem("sink_exp"), sem("exp_ready"), sem("denom"), sem("rcp_ready"), sem("probs_ready")
        pT_ready, pT_hi_ready, pT_lo_ready, pv_done = sem("pT_ready"), sem("pT_hi_ready"), sem("pT_lo_ready"), sem("pv_done")
        y_hi_ready, y_lo_ready = sem("y_hi_ready"), sem("y_lo_ready")
        gated, merged32, merged_hi, merged_lo = sem("gated"), sem("merged32"), sem("merged_hi"), sem("merged_lo")
        silu_ready, act_ready, a_hi_ready, a_lo_ready = sem("silu_ready"), sem("act_ready"), sem("a_hi_ready"), sem("a_lo_ready")
        out_sent = sem("out_sent")

        m_full = [sem(f"m_full{i}") for i in range(M_RAW)]
        m_hi_ready, m_lo_ready, m_done = sem("m_hi_ready"), sem("m_lo_ready"), sem("m_done")
        x_turned, x_copied = sem("x_turned"), sem("x_copied")
        logits_ready, logits_turned = sem("logits_ready"), sem("logits_turned")
        gap_ready, gap_exp = sem("gap_ready"), sem("gap_exp")
        route_consts, route_step, picks_ready, ranks_ready = sem("route_consts"), sem("route_step"), sem("picks_ready"), sem("ranks_ready")
        places_ready, lists_summed, lists_ready, counts_ready = sem("places_ready"), sem("lists_summed"), sem("lists_ready"), sem("counts_ready")
        pool_step = sem("pool_step")
        rows_in = sem("rows_in")
        h_row_sent = [sem("h_row_sent0"), sem("h_row_sent1")]
        xg_in = [sem("xg_in0"), sem("xg_in1")]
        xt_turned, xt_hi_ready, xt_lo_ready = sem("xt_turned"), sem("xt_hi_ready"), sem("xt_lo_ready")
        m_silu_ready, m_act_ready = sem("m_silu_ready"), sem("m_act_ready")
        at_turned, at_hi_ready, at_lo_ready = sem("at_turned"), sem("at_hi_ready"), sem("at_lo_ready")
        y_copied = sem("y_copied")
        y_sent = [sem("y_sent0"), sem("y_sent1")]
        stage_free = sem("stage_free")
        moe_done = sem("moe_done")
        y_back = [sem(f"y_back{t}") for t in range(TT)]
        mixed, mix_step, sq_ready, root_ready, inv_ready, scaled, pool_out, dve_out = sem("mixed"), sem("mix_step"), sem("sq_ready"), sem("root_ready"), sem("inv_ready"), sem("scaled"), sem("pool_out"), sem("dve_out")

        N_SMALL = 7

        def expert_units():
            for c, nb in enumerate(CHUNKS):
                for what in ("gate", "up"):
                    for j in range(4):
                        yield what, c, j, 2 * nb * P
            for f in range(KFE):
                yield "down", 0, f, D

        UNITS = list(expert_units())
        assert len(UNITS) == M_UNITS and M_UNITS % M_RAW == 0 and M_UNITS % M_SPL == 0
        CHUNK_END = {c: {w: max(u for u, x in enumerate(UNITS) if x[0] == w and x[1] == c) for w in ("gate", "up")}
                     for c in range(len(CHUNKS))}
        Y_BANKS = (6, 2)
        DOWN0 = M_UNITS - KFE
        TURN_LAST, TURN_X = DOWN0 + 1, (DOWN0 + 3, DOWN0 + 6)
        TURNED_AT = {CHUNK_END[0]["up"] + 1: 0, CHUNK_END[1]["up"] + 1: 1, TURN_LAST: 2}
        N_SEC = EXPERTS

        def step(s):
            hh, qb = s // TT, s % TT
            if hh < HEADS:
                return dict(hh=hh, qb=qb, a=True, q=4 + hh // 2, k=hh // 2, rows=HD * (hh % 2), v=hh // 2,
                            k0=0, nk=(qb + 1) * P)
            j, g = (hh - HEADS) // 2, hh % 2
            k0 = max(qb - 1, 0) * P
            return dict(hh=hh, qb=qb, a=False, q=8 + j, k=12, rows=HD * g, v=4, head=j + 4 * g,
                        k0=k0, nk=(qb + 1) * P - k0)

        def own_blocks(s):
            st = step(s)
            nb, q = st["nk"] // P, s % 2
            if st["qb"] < 2:
                return slice(q, q + 7 * (nb - 1) + 1, 7)
            b = 2 + 2 * (st["k0"] // P - (0 if st["a"] else 1)) + q
            return slice(b, b + 2 * (nb - 1) + 1, 2)

        def pair_products(p):
            if p % 2 == 0:
                return [(0, 0, 0, 2), (1, 8, 1, 1)]
            if step(2 * p)["a"]:
                return [(0, 2, 2, 2), (1, 4, 2, 2), (2, 6, 2, 2), (3, 9, 3, 1)]
            return [(2, 4, 2, 2), (1, 2, 2, 1), (3, 7, 3, 1)]

        THIRD = (MIX_START[0] + 2, MIX_START[1] + 2, FFN_START + 2)

        def split_of(n, c0, c1):
            if n not in THIRD:
                return w_hi[:, n % SPL, c0:c1], w_lo[:, n % SPL, c0:c1]
            if n == FFN_START + 2:
                parts = a_hi[:, KF - 2:KF, :], a_lo[:, KF - 2:KF, :]
            else:
                parts = kq_hi[:, N_PROJ - 2:, :], kq_lo[:, N_PROJ - 2:, :]
            return tuple(a.rearrange("p g t -> p (g t)")[:, c0:c1] for a in parts)

        def branch_banks(i):
            return (2, 4) if i % 2 == 0 else (6, 0)

        GATES_AT = {4 * g: g for g in range(N_GATE)}

        block = ctx.enter_context(nc.Block())

        @block.sync
        def _(sp):
            for k in range(KD):
                sp.dma_start(xs[:, k, :], xT[:, k, :]).then_inc(x_in[k], 16)
            sp.dma_start(gains[:, 0:DEPTH, :], g_mix).then_inc(small_in, 16)
            sp.dma_start(gains[:, DEPTH:2 * DEPTH, :], g_ffn).then_inc(small_in, 16)
            sp.dma_start(bg[:], b_gate).then_inc(small_in, 16)
            for layer in range(DEPTH):
                sp.dma_start(sink[:, layer, :], bass.AP(tensor=sinks.tensor, offset=layer * HEADS, ap=[[0, P], [1, HEADS]])).then_inc(small_in, 16)
                sp.dma_start(far[:, layer, :], bass.AP(tensor=rel_ext.tensor, offset=layer * HEADS * 384,
                                                       ap=[[0, P], [384, HEADS]]), allow_slow_non_contiguous=True).then_inc(small_in, 16)

            def load(n, src):
                if n >= RAW:
                    sp.wait_ge(lo_ready, n - RAW + 1)
                sp.dma_start(raw[:, n % RAW, 0:src.shape[1]], src).then_inc(raw_full[n % RAW], 16)

            for layer in range(DEPTH):
                n = MIX_START[layer]
                for u in range(U_BR):
                    load(n + u, w_in[layer, u])
                for i in range(N_BR // 2):
                    load(n + U_BR + 2 * i, w_a[layer, i])
                    load(n + U_BR + 2 * i + 1, w_b[layer, i])
                for u in range(N_OUT):
                    load(n + U_OUT + u, w_out[layer, u])
                if layer == 0:
                    for u in range(N_GU):
                        load(FFN_START + u, w_gu[u])
                    for u in range(N_DOWN):
                        c = 8 * (u % 3) * P
                        load(FFN_START + N_GU + u, w_down[u // 3, :, c:c + DOWN_TILES[u % 3] * P])
            load(U_ROUTER, w_router)
            sp.wait_ge(x_updated, 3 * KD)
            sp.dma_start(g_row[:], bass.AP(tensor=g_ffn_row.tensor, offset=0, ap=[[0, P], [1, D]])).then_inc(rows_in, 16)

            def expert_unit(e, u):
                what, c, j, cols = UNITS[u % M_UNITS]
                src = moe_down if what == "down" else moe_gu[c]
                row = j if what == "down" else 4 * (what == "up") + j
                sp.dma_start(m_raw[:, u % M_RAW, 0:cols], src[bass.ds(e, 1), row, :, :].rearrange("e p c -> p (e c)")
                             ).then_inc(m_full[u % M_RAW], 16)

            for u in range(M_RAW):
                expert_unit(0, u)

            def weights(first):
                with sp.Fori(0, N_SEC) as i:
                    following = (i + 1) % EXPERTS
                    for u in range(M_UNITS):
                        sp.wait_ge(m_lo_ready, i * M_UNITS + (first * M_UNITS + u + 1))
                        expert_unit(i if u + M_RAW < M_UNITS else following, u + M_RAW)

            weights(0)
            sp.wait_ge(h_row_sent[0], 16 * 3)
            sp.wait_ge(h_row_sent[1], 16 * 2)
            sp.dma_start(gf_row, bass.AP(tensor=g_final_row.tensor, offset=0, ap=[[0, P], [1, D]])).then_inc(rows_in, 16)
            sp.wait_ge(counts_ready, 1)
            with sp.If(sp.value_load(most[0:1, 0:1], min_val=0, max_val=T) > CAP):
                weights(N_SEC)
            sp.wait_ge(moe_done, 1)
            for t in range(TT):
                sp.dma_start(y_of(t), y_dram[2 * t * P:2 * (t + 1) * P, :].rearrange("(p c) d -> p c d", c=2)
                             ).then_inc(y_back[t], 16)
            for t in range(TT):
                if t < 2:
                    sp.wait_ge(pool_out, t + 1)
                else:
                    sp.wait_ge(dve_out, t - 1)
                sp.dma_start(out[t * P:(t + 1) * P, :], x_rows[:, t, :]).then_inc(out_sent, 16)
            sp.wait_ge(out_sent, 16 * TT)

        @block.gpsimd
        def _(pool):
            pool.memset(idle[:], 0.0)
            pool.memset(eps[:], EPS).then_inc(basics, 1)
            pool.memset(ident[:], 0.0).then_inc(const_step, 1)
            pool.memset(ones[:], 1.0)
            pool.memset(mean_of[:], 1.0 / D).then_inc(basics, 1)
            pool.wait_ge(const_step, 1)
            pool.affine_select(out=ident[:], in_=ident[:], compare_op=ALU.not_equal, fill=1.0, base=0,
                               pattern=[[-1, P]], channel_multiplier=1).then_inc(basics, 1)
            pool.memset(flip, 0.0).then_inc(const_step, 1)
            pool.wait_ge(const_step, 2)
            pool.affine_select(out=flip, in_=flip, compare_op=ALU.not_equal, fill=1.0, base=1 - P,
                               pattern=[[1, P]], channel_multiplier=1).then_inc(consts, 1)
            pool.iota(alibi[:], [[-1, 2 * P]], base=2 * P - 1, channel_multiplier=-1,
                      allow_small_or_imprecise_dtypes=True).then_inc(const_step, 1)
            pool.wait_ge(const_step, 3)
            pool.memset(alibi[0:HD, 0:2 * HD], -MASKED).then_inc(const_step, 1)
            pool.wait_ge(const_step, 4)
            pool.memset(alibi[HD:P, 0:HD], -MASKED).then_inc(const_step, 1)
            pool.wait_ge(const_step, 5)
            pool.memset(alibi[HD:P, 3 * HD:4 * HD], -MASKED).then_inc(const_step, 1)
            pool.wait_ge(const_step, 6)
            pool.sem_inc(consts, 1)
            for i in range(DEPTH * HEADS):
                if i % HEADS:
                    pool.wait_ge(bias_lo_ready, i)
                else:
                    pool.wait_ge(h_lo_ready, (2 * (i // HEADS) + 1) * KD)
                pool.dma_start(bias[:], bass.AP(tensor=rel_ext.tensor, offset=i * 384, ap=[[1, P], [1, 2 * P]])).then_inc(bias_in, 16)
                pool.wait_ge(bias_in, 16 * (i + 1))
                pool.memset(bias[HD:P, 3 * HD:4 * HD], MASKED).then_inc(bias_masked, 1)
            steps = [0]

            def one(ins):
                steps[0] += 1
                ins.then_inc(pool_step, 1)
                pool.wait_ge(pool_step, steps[0])

            pool.wait_ge(bias_masked, DEPTH * HEADS)
            pool.wait_ge(x_updated, 3 * KD)
            one(pool.memset(all_ones[:], 1.0))
            one(pool.memset(before[:], 1.0))
            one(pool.affine_select(out=before[:], in_=before[:], compare_op=ALU.is_gt, fill=0.0, base=0,
                                   pattern=[[1, P]], channel_multiplier=-1))
            one(pool.iota(rt[:, 0, :, :], [[0, TT], [-1, EXPERTS]], base=EXPERTS, channel_multiplier=0,
                          allow_small_or_imprecise_dtypes=True))
            one(pool.iota(rt[:, 1, :, :], [[0, TT], [SLOTS, EXPERTS]], base=0, channel_multiplier=0,
                          allow_small_or_imprecise_dtypes=True))
            for c in range(2):
                mine = slice(c * TT, (c + 1) * TT)
                one(pool.iota(entry[:, mine, 0], [[P, TT]], base=-PAD_H, channel_multiplier=1, allow_small_or_imprecise_dtypes=True))
                one(pool.iota(entry[:, mine, 1], [[2 * P, TT]], base=c - PAD_Y, channel_multiplier=2, allow_small_or_imprecise_dtypes=True))
            one(pool.iota(numbers[:], [[1, P]], base=0, channel_multiplier=0, allow_small_or_imprecise_dtypes=True))
            pool.sem_inc(route_consts, 1)
            one(pool.memset(zeros[:], 0.0))
            pool.dma_start(h_dram[T:T + 1, :], zeros[:]).then_inc(h_row_sent[0], 16)
            pool.wait_ge(rows_in, 16)
            for t in range(TT):
                pool.wait_ge(x_copied, t + 1)
                one(pool.tensor_tensor(h_rows[:, t, :], h_rows[:, t, :], g_row[:], ALU.mult))
                pool.dma_start(h_dram[t * P:(t + 1) * P, :], h_rows[:, t, :]).then_inc(h_row_sent[t % 2], 16)
            pool.wait_ge(lists_ready, 1)
            pool.wait_ge(h_row_sent[0], 16 * 3)
            pool.wait_ge(h_row_sent[1], 16 * 2)

            def where_used(p, sl, second_round, move):
                if second_round or (p < N_SEC and sl == 0):
                    move(P)
                    return
                used = (counts[0:1, p:p + 1], P) if p < N_SEC else (most[0:1, 0:1], CAP)
                with pool.If(pool.value_load(used[0], min_val=0, max_val=T) > used[1]):
                    move(P)
                with pool.Else():
                    move(2)

            def gather(p, second_round=False):
                for sl in range(SLOTS):
                    where_used(p, sl, second_round or p == 0, lambda n: pool.indirect_dma_start(
                        out=xg[0:n, sl, :], out_offset=None, in_=h_dram,
                        in_offset=bass.IndirectOffsetOnAxis(ap=lists[0:n, SLOTS * p + sl, 0:1], axis=0)).then_inc(xg_in[sl], 16))

            def moves(first):
                for p in range(first, first + N_SEC):
                    for sl in range(SLOTS):
                        pool.wait_ge(xg_in[sl], 16 * (p + 2))
                    pool.wait_ge(xt_turned, 4 * (p + 2))
                    gather(min(p + 2, 2 * N_SEC - 1), second_round=first > 0)
                    for sl in range(SLOTS):
                        if p:
                            pool.wait_ge(y_sent[sl], 16 * p)
                        pool.sem_inc(stage_free, 1)
                    for sl in range(SLOTS):
                        pool.wait_ge(y_copied, SLOTS * p + SLOTS + sl + 1)
                        where_used(p, sl, first > 0, lambda n: pool.indirect_dma_start(
                            out=y_dram, out_offset=bass.IndirectOffsetOnAxis(ap=lists[0:n, SLOTS * p + sl, 1:2], axis=0),
                            in_=(y_stage if n == P else x_rows)[0:n, sl, :], in_offset=None, bounds_check=2 * T - 1, oob_is_err=False).then_inc(y_sent[sl], 16))
                for sl in range(SLOTS):
                    pool.wait_ge(y_sent[sl], 16 * (first + N_SEC))
                    pool.wait_ge(xg_in[sl], 16 * (first + N_SEC + 2))

            gather(0)
            pool.wait_ge(xg_in[0], 16)
            pool.wait_ge(xg_in[1], 16)
            pool.wait_ge(xt_turned, 4)
            gather(1)
            moves(0)
            with pool.If(pool.value_load(most[0:1, 0:1], min_val=0, max_val=T) > CAP):
                moves(N_SEC)
            pool.sem_inc(moe_done, 1)
            pool.wait_ge(rows_in, 32)
            for t in range(2):
                pool.wait_ge(scaled, t + 1)
                pool.tensor_tensor(x_rows[:, t, :], x_rows[:, t, :], gf_row, ALU.mult).then_inc(pool_out, 1)

        @block.scalar
        def _(act_):
            A = act_

            def split_hi(n, cols=UNIT):
                A.wait_ge(raw_full[n % RAW], 16 * (n // RAW + 1))
                if n >= SPL and n not in THIRD:
                    A.wait_ge(unit_done, n - SPL + 1)
                A.activation(split_of(n, 0, cols)[0], raw[:, n % RAW, 0:cols], ACT.Copy).then_inc(hi_ready, 1)

            def square(i, k):
                if i < KD:
                    A.wait_ge(x_in[k], 16)
                else:
                    A.wait_ge(x_updated, i - KD + 1)
                if i >= 2:
                    A.wait_ge(summed, i - 1)
                A.activation(ps[:, SQ_BANK + i % 2, :], xs[:, k, :], ACT.Square).then_inc(squared, 1)

            def warm_root():
                A.activation(warm[:], eps[:], ACT.Sqrt)

            def root(j):
                A.wait_ge(mean_ready, j + 1)
                A.activation(root_[:], ps[:, SUM_BANK, 0:TT], ACT.Sqrt, bias=eps[:, 0:1]).then_inc(norm_root, 1)

            def bias_split(H):
                layer, hh = H // (2 * HEADS), H % (2 * HEADS)
                if H >= 2:
                    A.wait_ge(scores_ready, TT * (H - 1))
                if hh < HEADS:
                    A.wait_ge(bias_masked, layer * HEADS + hh + 1)
                    A.activation(bias_hi[:, H % 2, :], bias, ACT.Identity, bias=nfar[:, layer, hh:hh + 1]).then_inc(bias_hi_ready, 1)
                else:
                    A.activation(bias_hi[:, H % 2, :], alibi[:], ACT.Copy,
                                 scale=-2.0 ** -(step(TT * hh)["head"] + 1)).then_inc(bias_hi_ready, 1)

            def x_copy(t):
                A.wait_ge(x_turned, t + 1)
                rows = ps[:, 0:2, :].rearrange("p b c -> p (b c)")
                A.activation(x_rows[:, t, :], rows, ACT.Copy)
                A.activation(h_rows[:, t, :], rows, ACT.Copy, scale=rinv[:, 3, t:t + 1]).then_inc(x_copied, 1)

            def h_split(i):
                A.wait_ge(h32_ready, i + 1)
                A.activation(h_hi[:, i % KD, :], ps[:, H32_BANK + i % 2, :], ACT.Copy).then_inc(h_hi_ready, 1)

            A.wait_ge(basics, 1)
            warm_root()
            for k in range(KD):
                square(k, k)
            for layer in range(DEPTH):
                n0 = MIX_START[layer]
                norm_i = 2 * layer
                root(norm_i)
                if layer == 0:
                    split_hi(0)
                    split_hi(1)
                for k in range(KD):
                    h_split(norm_i * KD + k)
                split_hi(n0 + 2)
                if layer == 0:
                    A.wait_ge(consts, 4)
                    A.activation(flip_r[:], flip, ACT.Copy).then_inc(flip_ready, 1)
                for u in range(N_PROJ):
                    n = n0 + u
                    A.wait_ge(unit_done, n + 1)
                    if u:
                        split_hi(n + 2)
                    A.activation(kq_hi[:, u, :], ps[:, n % 2, :], ACT.Copy,
                                 scale=SCALE if 4 <= u < 12 else 1.0).then_inc(kq_hi_ready, 1)
                for u in range(N_V + 1):
                    n = n0 + U_V + u
                    if u < N_V:
                        A.wait_ge(unit_done, n + 1)
                        split_hi(n + 2)
                        i = layer * N_V + u
                        if i >= 2:
                            A.wait_ge(vT_turned, i - 1)
                        A.activation(probs[:, i % 2, :], ps[:, n % 2, :], ACT.Copy).then_inc(vT_copied, 1)
                    if u >= 1:
                        i = layer * N_V + u - 1
                        A.wait_ge(vT_turned, i + 1)
                        A.activation(v_hi[:, :, (u - 1) * P:u * P],
                                     ps[:, T_BANK + i % 2, :].rearrange("p (t c) -> p t c", c=P),
                                     ACT.Copy).then_inc(v_hi_ready, 1)

                bias_split(layer * 2 * HEADS)
                for tick in range(STEPS + 5):
                    if 2 <= tick < STEPS + 2:
                        s, st = layer * STEPS + tick - 2, step(tick - 2)
                        A.wait_ge(pT_ready, s + 1)
                        if s >= 4:
                            A.wait_ge(pv_done, s // 2 - 1)
                        A.activation(pT_hi[:, own_blocks(tick - 2), :],
                                     ps[:, T_BANK + s % 2, 0:st["nk"]].rearrange("p (b c) -> p b c", c=P),
                                     ACT.Copy).then_inc(pT_hi_ready, 1)
                    if tick < STEPS:
                        s, st = layer * STEPS + tick, step(tick)
                        A.wait_ge(nmax_ready, s + 1)
                        c = s % 4
                        if not st["a"]:
                            A.activation(stat[:, 3, c:c + 1], sink[:, layer, st["head"]:st["head"] + 1], ACT.Exp,
                                         bias=stat[:, 1, c:c + 1]).then_inc(sink_exp, 1)
                        A.activation(probs[:, s % 2, 0:st["nk"]], ps[:, S_BANK + s % 2, 0:st["nk"]], ACT.Exp,
                                     bias=stat[:, 1, c:c + 1], accum_out=stat[:, 2, c:c + 1]).then_inc(exp_ready, 1)
                    if tick % TT == 1 and tick < STEPS - TT:
                        bias_split(layer * 2 * HEADS + tick // TT + 1)
                    if (tick - 4) in GATES_AT:
                        g = GATES_AT[tick - 4]
                        n = n0 + U_GATE + g
                        A.wait_ge(unit_done, n + 1)
                        split_hi(n + 2)
                        A.activation(gates[:, g, :], ps[:, n % 2, :], ACT.Tanh, scale=0.5,
                                     bias=bg[:, layer, g:g + 1]).then_inc(drained_act, 1)
                    if tick >= 8 and tick % 4 == 0:
                        hh = (tick - 8) // 4
                        H = layer * 2 * HEADS + hh
                        st = step(4 * hh)
                        r = st["rows"]
                        A.wait_ge(pv_done, 2 * (H + 1))
                        A.activation(kq_hi[r:r + HD, st["q"], :], ps[r:r + HD, O_BANK + hh % 2, :],
                                     ACT.Copy).then_inc(y_hi_ready, 1)

                for i in range(N_BR // 2):
                    n = n0 + U_BR + 2 * i
                    A.wait_ge(unit_done, n + 1)
                    split_hi(n + 2)
                    A.wait_ge(unit_done, n + 2)
                    split_hi(n + 3)
                    for mm in range(2):
                        m = layer * KD + 2 * i + mm
                        A.wait_ge(merged32, m + 1)
                        A.activation(h_hi[:, 2 * i + mm, :], probs[:, 0, :], ACT.Copy, scale=0.5).then_inc(merged_hi, 1)
                last = n0 + N_MIX
                warm_root()
                for u in range(N_OUT):
                    n = n0 + U_OUT + u
                    A.wait_ge(unit_done, n + 1)
                    if layer == 0 or n + 2 <= last:
                        split_hi(n + 2)
                    square((norm_i + 1) * KD + u, u)
                root(norm_i + 1)
                if layer == 1:
                    A.wait_ge(rinv_ready, 4)
                    x_copy(0)
                for k in range(KD):
                    h_split((norm_i + 1) * KD + k)
                    if layer == 1 and k in (1, 3, 5):
                        x_copy((k + 1) // 2)
                if layer == 0:
                    split_hi(FFN_START + 2)
                    for u in range(N_GU):
                        n = FFN_START + u
                        A.wait_ge(unit_done, n + 1)
                        if u:
                            split_hi(n + 2)
                        f = u // 2
                        if u % 2 == 0:
                            if f >= 2:
                                A.wait_ge(act_ready, f - 1)
                            A.activation(silu[:, f % 2, :], ps[:, n % 2, :], ACT.Silu).then_inc(silu_ready, 1)
                        else:
                            A.wait_ge(act_ready, f + 1)
                            A.activation(a_hi[:, f, :], act[:, f % 2, :], ACT.Copy).then_inc(a_hi_ready, 1)
                    warm_root()
                    for u in range(N_DOWN):
                        n = FFN_START + N_GU + u
                        A.wait_ge(unit_done, n + 1)
                        if (u + 2) % 3 == 2 and u + 2 < N_DOWN:
                            split_hi(n + 2, DOWN_TILES[2] * P)
                        else:
                            split_hi(n + 2)
                        if u % 3 == 2:
                            square(2 * KD + u // 3, u // 3)

            A.sem_inc(m_silu_ready, SLOTS)
            A.sem_inc(y_copied, SLOTS)
            A.wait_ge(unit_done, U_ROUTER + 1)
            A.activation(logits_T, ps[:, 3, :], ACT.Copy).then_inc(logits_ready, 1)
            A.wait_ge(gap_ready, 1)
            A.activation(r1[:, 3, :], r1[:, 2, :], ACT.Exp).then_inc(gap_exp, 1)

            def expert_hi(full, u):
                A.wait_ge(m_full[u % M_RAW], full)
                cols = UNITS[u % M_UNITS][3]
                A.activation(m_hi[:, u % M_SPL, 0:cols], m_raw[:, u % M_RAW, 0:cols], ACT.Copy).then_inc(m_hi_ready, 1)

            def turned_x(done, sl):
                for hb in range(2):
                    A.wait_ge(xt_turned, done + (2 * sl + hb + 1))
                    A.activation(xt_hi[:, 4 * hb:4 * hb + 4, sl, :], ps[:, hb, :].rearrange("p (k c) -> p k c", c=P),
                                 ACT.Copy).then_inc(xt_hi_ready, 1)

            for u in range(M_SPL):
                expert_hi(16, u)
            turned_x(0, 0)
            turned_x(0, 1)

            def passes(first, always_both):
                with A.Fori(0, N_SEC) as i:
                    def pass_of(slots):
                        for u in range(M_UNITS):
                            A.wait_ge(m_done, i * M_UNITS + (first * M_UNITS + u + 1))
                            v = u + M_SPL
                            expert_hi(i * (16 * (M_UNITS // M_RAW)) + 16 * (first * (M_UNITS // M_RAW) + v // M_RAW + 1), v)
                            for c in range(len(CHUNKS)):
                                if u == CHUNK_END[c]["gate"]:
                                    w = CHUNKS[c] * P
                                    for sl in range(slots):
                                        A.wait_ge(m_act_ready, i * 6 + (6 * first + 2 * c + sl + 1))
                                        A.activation(m_silu[:, sl, 0:w], ps[:, sl, 0:w], ACT.Silu).then_inc(m_silu_ready, SLOTS // slots)
                            if u in TURNED_AT:
                                c = TURNED_AT[u]
                                nb = CHUNKS[c]
                                for sl in range(slots):
                                    A.wait_ge(at_turned, i * 6 + (6 * first + SLOTS + 2 * c + sl + 1))
                                    A.activation(at_hi[:, 4 * c:4 * c + nb, sl, :],
                                                 ps[:, 4 + sl, 0:nb * P].rearrange("p (k c) -> p k c", c=P),
                                                 ACT.Copy).then_inc(at_hi_ready, SLOTS // slots)
                            if u in TURN_X:
                                turned_x(i * 4 + 4 * (first + 1), TURN_X.index(u))
                        for sl in range(slots):
                            A.wait_ge(stage_free, i * SLOTS + (SLOTS * first + sl + 1))
                            A.activation(y_stage[:, sl, :], ps[:, Y_BANKS[sl]:Y_BANKS[sl] + 2, :].rearrange("p b c -> p (b c)"),
                                         ACT.Copy).then_inc(y_copied, SLOTS // slots)

                    if always_both:
                        pass_of(SLOTS)
                    else:
                        with A.If(A.value_load(counts[0:1, bass.ds(i, 1)], min_val=0, max_val=T) > P):
                            pass_of(SLOTS)
                        with A.Else():
                            pass_of(1)

            A.wait_ge(counts_ready, 1)
            passes(0, False)
            with A.If(A.value_load(most[0:1, 0:1], min_val=0, max_val=T) > CAP):
                passes(N_SEC, True)
            warm_root()
            for t in range(TT):
                A.wait_ge(mixed, t + 1)
                A.activation(ps[:, 0:2, :].rearrange("p b c -> p (b c)"), x_rows[:, t, :], ACT.Square, accum_out=r1[:, 8, t:t + 1]).then_inc(sq_ready, 1)
                A.wait_ge(sq_ready, t + 1)
                A.activation(r1[:, 9, t:t + 1], r1[:, 8, t:t + 1], ACT.Sqrt, scale=1.0 / D, bias=eps[:, 0:1]).then_inc(root_ready, 1)
                if 1 <= t <= 2:
                    A.wait_ge(inv_ready, t)
                    A.activation(x_rows[:, t - 1, :], x_rows[:, t - 1, :], ACT.Copy, scale=r1[:, 6, t - 1:t]).then_inc(scaled, 1)

        @block.vector
        def _(V):
            def split_lo(n, cols=UNIT):
                V.wait_ge(hi_ready, n + 1)
                hi, lo = split_of(n, 0, cols)
                V.tensor_tensor(lo, raw[:, n % RAW, 0:cols], hi.bitcast(F32), ALU.subtract).then_inc(lo_ready, 1)

            def lo_of(out, full, hi):
                return V.tensor_tensor(out, full, hi.bitcast(F32), ALU.subtract)

            def sum_squares(i, k):
                V.wait_ge(squared, i + 1)
                if k == 0:
                    if i:
                        V.wait_ge(h32_ready, i)
                    V.tensor_copy(norm[:], ps[:, SQ_BANK + i % 2, :]).then_inc(summed, 1)
                else:
                    V.wait_ge(summed, i)
                    V.tensor_tensor(norm[:], norm[:], ps[:, SQ_BANK + i % 2, :], ALU.add).then_inc(summed, 1)

            def rms(j, gi):
                V.wait_ge(norm_root, j + 1)
                V.reciprocal(rinv[:, j, :], root_[:]).then_inc(rinv_ready, 1)
                V.wait_ge(rinv_ready, j + 1)
                V.tensor_tensor(norm[:].rearrange("p (t c) -> p t c", c=P), ident[:].unsqueeze(1).to_broadcast([P, TT, P]),
                                rinv[:, j, :].unsqueeze(2).to_broadcast([P, TT, P]), ALU.mult).then_inc(diag_ready, 1)
                if j == 0:
                    split_lo(0)
                    split_lo(1)
                V.wait_ge(rinv_spread, j + 1)
                for k in range(KD + 1):
                    i = j * KD + k
                    if k < KD:
                        if k >= 2:
                            V.wait_ge(h_lo_ready, i - 1)
                        V.scalar_tensor_tensor(out=ps[:, H32_BANK + i % 2, :], in0=xs[:, k, :],
                                               scalar=gains[:, gi, k:k + 1], in1=ps[:, SUM_BANK, :],
                                               op0=ALU.mult, op1=ALU.mult).then_inc(h32_ready, 1)
                    if k >= 1:
                        V.wait_ge(h_hi_ready, i)
                        lo_of(h_lo[:, k - 1, :], ps[:, H32_BANK + (i - 1) % 2, :], h_hi[:, k - 1, :]).then_inc(h_lo_ready, 1)

            def small_consts():
                V.wait_ge(small_in, 16 * N_SMALL)
                V.tensor_scalar(bg[:], bg[:], 0.5, None, ALU.mult)
                V.tensor_scalar(nfar[:], far[:], -1.0, None, ALU.mult)
                V.tensor_scalar(nsink[:], sink[:], -1.0, None, ALU.mult).then_inc(consts, 1)
                V.wait_ge(consts, 3)
                V.scalar_tensor_tensor(out=alibi[:], in0=alibi[:], scalar=-1.0, in1=alibi[:], op0=ALU.mult,
                                       op1=ALU.max).then_inc(consts, 1)
                V.wait_ge(consts, 4)

            for k in range(KD):
                sum_squares(k, k)
            small_consts()
            for layer in range(DEPTH):
                n0 = MIX_START[layer]
                norm_i = 2 * layer
                rms(norm_i, layer)
                for u in range(N_PROJ):
                    n = n0 + u
                    split_lo(n + 2)
                    V.wait_ge(kq_hi_ready, layer * N_PROJ + u + 1)
                    V.scalar_tensor_tensor(out=kq_lo[:, u, :], in0=ps[:, n % 2, :], scalar=SCALE if 4 <= u < 12 else 1.0,
                                           in1=kq_hi[:, u, :].bitcast(F32), op0=ALU.mult,
                                           op1=ALU.subtract).then_inc(drained_dve, 1)
                for u in range(N_V + 1):
                    if u < N_V:
                        split_lo(n0 + U_V + u + 2)
                    if u >= 1:
                        i = layer * N_V + u - 1
                        V.wait_ge(v_hi_ready, i + 1)
                        lo_of(v_lo[:, :, (u - 1) * P:u * P],
                              ps[:, T_BANK + i % 2, :].rearrange("p (t c) -> p t c", c=P),
                              v_hi[:, :, (u - 1) * P:u * P]).then_inc(v_lo_ready, 1)

                def bias_split(hh):
                    if hh < HEADS:
                        H = layer * 2 * HEADS + hh
                        V.wait_ge(bias_hi_ready, H + 1)
                        V.scalar_tensor_tensor(out=bias_lo[:, H % 2, :], in0=bias, scalar=nfar[:, layer, hh:hh + 1],
                                               in1=bias_hi[:, H % 2, :].bitcast(F32), op0=ALU.add,
                                               op1=ALU.subtract).then_inc(bias_lo_ready, 1)

                bias_split(0)
                for tick in range(STEPS + 5):
                    if tick < STEPS:
                        s, st = layer * STEPS + tick, step(tick)
                        c, nk, sc = s % 4, st["nk"], ps[:, S_BANK + s % 2, :]
                        V.wait_ge(scores_ready, s + 1)
                        if st["a"]:
                            V.tensor_reduce(stat[:, 1, c:c + 1], sc[:, 0:nk], AX.X, ALU.max, negate=True).then_inc(nmax_ready, 1)
                        else:
                            V.tensor_reduce(stat[:, 0, c:c + 1], sc[:, 0:nk], AX.X, ALU.max, negate=True).then_inc(max_ready, 1)
                            V.wait_ge(max_ready, layer * STEPS // 2 + tick + 1 - STEPS // 2)
                            V.tensor_tensor(stat[:, 1, c:c + 1], stat[:, 0, c:c + 1],
                                            nsink[:, layer, st["head"]:st["head"] + 1], ALU.min).then_inc(nmax_ready, 1)
                    if 1 <= tick < STEPS + 1:
                        s, st = layer * STEPS + tick - 1, step(tick - 1)
                        c, nk, t = s % 4, st["nk"], probs[:, s % 2, :]
                        V.wait_ge(exp_ready, s + 1)
                        den = stat[:, 2, c:c + 1]
                        if not st["a"]:
                            V.tensor_tensor(stat[:, 4, c:c + 1], den, stat[:, 3, c:c + 1], ALU.add).then_inc(denom, 1)
                            V.wait_ge(denom, layer * STEPS // 2 + tick - STEPS // 2)
                            den = stat[:, 4, c:c + 1]
                        V.reciprocal(stat[:, 5, c:c + 1], den).then_inc(rcp_ready, 1)
                        V.wait_ge(rcp_ready, s + 1)
                        V.tensor_scalar(t[:, 0:nk], t[:, 0:nk], stat[:, 5, c:c + 1], None, ALU.mult).then_inc(probs_ready, 1)
                    if 2 <= tick < STEPS + 2:
                        s, st = layer * STEPS + tick - 2, step(tick - 2)
                        nk = st["nk"]
                        V.wait_ge(pT_hi_ready, s + 1)
                        mine = own_blocks(tick - 2)
                        lo_of(pT_lo[:, mine, :], ps[:, T_BANK + s % 2, 0:nk].rearrange("p (b c) -> p b c", c=P),
                              pT_hi[:, mine, :]).then_inc(pT_lo_ready, 1)
                    if tick % TT == 1 and tick < STEPS - TT:
                        bias_split(tick // TT + 1)
                    if (tick - 4) in GATES_AT:
                        split_lo(n0 + U_GATE + GATES_AT[tick - 4] + 2)
                    if tick >= 8 and tick % 4 == 0:
                        hh = (tick - 8) // 4
                        H = layer * 2 * HEADS + hh
                        st = step(4 * hh)
                        r = st["rows"]
                        V.wait_ge(y_hi_ready, H + 1)
                        lo_of(kq_lo[r:r + HD, st["q"], :], ps[r:r + HD, O_BANK + hh % 2, :],
                              kq_hi[r:r + HD, st["q"], :]).then_inc(y_lo_ready, 1)

                for i in range(N_BR // 2):
                    n = n0 + U_BR + 2 * i
                    split_lo(n + 2)
                    split_lo(n + 3)
                    V.wait_ge(unit_done, n + 2)
                    V.wait_ge(drained_act, N_GATE * (layer + 1))
                    for mm in range(2):
                        m = layer * KD + 2 * i + mm
                        za, zb = branch_banks(i)
                        if m:
                            V.wait_ge(merged_lo, m)
                        V.scalar_tensor_tensor(out=probs[:, 1, :], in0=gates[:, 2 * (2 * i + mm) + 1, :], scalar=1.0,
                                               in1=ps[:, zb + mm, :], op0=ALU.add, op1=ALU.mult)
                        V.scalar_tensor_tensor(out=probs[:, 0, :], in0=gates[:, 2 * (2 * i + mm), :], scalar=1.0,
                                               in1=ps[:, za + mm, :], op0=ALU.add, op1=ALU.mult).then_inc(gated, 1)
                        V.wait_ge(gated, m + 1)
                        V.tensor_tensor(probs[:, 0, :], probs[:, 0, :], probs[:, 1, :], ALU.add).then_inc(merged32, 1)
                        V.wait_ge(merged_hi, m + 1)
                        V.scalar_tensor_tensor(out=h_lo[:, 2 * i + mm, :], in0=probs[:, 0, :], scalar=0.5,
                                               in1=h_hi[:, 2 * i + mm, :].bitcast(F32), op0=ALU.mult,
                                               op1=ALU.subtract).then_inc(merged_lo, 1)
                last = n0 + N_MIX
                for u in range(N_OUT):
                    n = n0 + U_OUT + u
                    if layer == 0 or n + 2 <= last:
                        split_lo(n + 2)
                    V.wait_ge(unit_done, n + 1)
                    V.tensor_tensor(xs[:, u, :], xs[:, u, :], ps[:, T_BANK + n % 2, :], ALU.add).then_inc(x_updated, 1)
                    sum_squares((norm_i + 1) * KD + u, u)
                rms(norm_i + 1, DEPTH + layer)
                if layer == 0:
                    for u in range(N_GU):
                        n = FFN_START + u
                        split_lo(n + 2)
                        f = u // 2
                        if u % 2 == 1:
                            V.wait_ge(silu_ready, f + 1)
                            V.wait_ge(unit_done, n + 1)
                            if f >= 2:
                                V.wait_ge(a_lo_ready, f - 1)
                            V.tensor_tensor(act[:, f % 2, :], silu[:, f % 2, :], ps[:, n % 2, :], ALU.mult).then_inc(act_ready, 1)
                            V.wait_ge(a_hi_ready, f + 1)
                            lo_of(a_lo[:, f, :], act[:, f % 2, :], a_hi[:, f, :]).then_inc(a_lo_ready, 1)
                    for u in range(N_DOWN):
                        n = FFN_START + N_GU + u
                        if (u + 2) % 3 == 2 and u + 2 < N_DOWN:
                            split_lo(n + 2, DOWN_TILES[2] * P)
                        else:
                            split_lo(n + 2)
                        if u % 3 == 2:
                            m = u // 3
                            V.wait_ge(unit_done, n + 1)
                            V.tensor_tensor(xs[:, m, :], xs[:, m, :], ps[:, m % 2, :], ALU.add).then_inc(x_updated, 1)
                            sum_squares(2 * KD + m, m)

            V.sem_inc(m_act_ready, SLOTS)
            V.sem_inc(at_lo_ready, SLOTS)
            steps = [0]

            def link(ins):
                steps[0] += 1
                ins.then_inc(route_step, 1)
                V.wait_ge(route_step, steps[0])

            def each(a):
                return a.unsqueeze(2).to_broadcast([P, TT, EXPERTS])

            V.wait_ge(route_consts, 1)
            rank8, twice_e, lg, hit, key, first_, second, rest = (rt[:, j, :, :] for j in range(8))
            both, of_both, of_both_e = rt[:, 5:7, :, :], rt[:, 8:10, :, :], rt[:, 10:12, :, :]
            V.wait_ge(logits_turned, 1)
            link(V.tensor_copy(lg, ps[:, 2, :].rearrange("p (t c) -> p t c", c=P)[:, :, 0:EXPERTS]))

            def largest(values, chosen, top):
                link(V.tensor_reduce(top, values, AX.X, ALU.max))
                link(V.tensor_tensor(hit, values, each(top), ALU.is_equal))
                link(V.tensor_tensor(key, hit, rank8, ALU.mult))
                link(V.tensor_reduce(r1[:, 6, :], key, AX.X, ALU.max))
                link(V.tensor_tensor(chosen, key, each(r1[:, 6, :]), ALU.is_equal))

            largest(lg, first_, r1[:, 0, :])
            link(V.scalar_tensor_tensor(out=rest, in0=first_, scalar=-3.0e38, in1=lg, op0=ALU.mult, op1=ALU.add))
            largest(rest, second, r1[:, 1, :])
            V.tensor_tensor(picks[:], first_, second, ALU.add).then_inc(picks_ready, 1)
            V.tensor_tensor(r1[:, 2, :], r1[:, 1, :], r1[:, 0, :], ALU.subtract).then_inc(gap_ready, 1)
            rank, col, row, past1, past2, past3, times, col0 = (spot[:, j, :] for j in range(8))
            link(V.tensor_tensor(of_both_e, both, twice_e.unsqueeze(1).to_broadcast([P, 2, TT, EXPERTS]), ALU.mult))
            link(V.tensor_reduce(col0, of_both_e, AX.X, ALU.add))
            V.wait_ge(ranks_ready, 1)
            ranks = ps[:, 3, 0:TT * EXPERTS].rearrange("p (t e) -> p t e", e=EXPERTS)
            link(V.tensor_tensor(of_both, both, ranks.unsqueeze(1).to_broadcast([P, 2, TT, EXPERTS]), ALU.mult))
            link(V.tensor_reduce(rank, of_both, AX.X, ALU.add))
            for j, past in enumerate((past1, past2)):
                V.tensor_scalar(past, rank, float((j + 1) * P), None, ALU.is_ge)
            link(V.tensor_scalar(past3, rank, float(3 * P), None, ALU.is_ge))
            V.scalar_tensor_tensor(out=col, in0=past2, scalar=float(SLOTS * EXPERTS - 2), in1=col0, op0=ALU.mult, op1=ALU.add)
            link(V.tensor_tensor(times, past1, past2, ALU.add))
            link(V.tensor_tensor(times, times, past3, ALU.add))
            V.tensor_tensor(col, col, times, ALU.add)
            link(V.scalar_tensor_tensor(out=row, in0=times, scalar=-float(P), in1=rank, op0=ALU.mult, op1=ALU.add))
            link(V.tensor_tensor(in_column[:], numbers[:, 0:LISTS].unsqueeze(1).to_broadcast([P, 2 * TT, LISTS]),
                                 col.unsqueeze(2).to_broadcast([P, 2 * TT, LISTS]), ALU.is_equal))
            for c in range(2):
                mine = slice(c * TT, (c + 1) * TT)
                V.tensor_tensor(entry_hit[:, mine, :, :], in_column[:, mine, :].unsqueeze(3).to_broadcast([P, TT, LISTS, 2]),
                                entry[:, mine, :].unsqueeze(2).to_broadcast([P, TT, LISTS, 2]), ALU.mult)
                V.tensor_tensor(row_hit[:, mine, :], numbers[:].unsqueeze(1).to_broadcast([P, TT, P]),
                                row[:, mine].unsqueeze(2).to_broadcast([P, TT, P]), ALU.is_equal).then_inc(places_ready, 1)
            V.tensor_copy(counts[:], ps[:, 3, 64:64 + EXPERTS])
            link(V.tensor_reduce(most[:], ps[:, 3, 64:64 + EXPERTS], AX.X, ALU.max))
            V.sem_inc(counts_ready, 1)
            V.wait_ge(lists_summed, 1)
            sums = ps[:, 2, 0:2 * LISTS].rearrange("p (c i) -> p c i", i=2)
            V.tensor_scalar(lists[:, :, 0], sums[:, :, 0], float(PAD_H), None, ALU.add)
            link(V.tensor_scalar(lists[:, :, 1], sums[:, :, 1], float(PAD_Y), None, ALU.add))
            V.sem_inc(lists_ready, 1)
            V.wait_ge(gap_exp, 1)
            link(V.tensor_scalar(r1[:, 2, :], r1[:, 3, :], 1.0, None, ALU.add))
            link(V.reciprocal(r1[:, 4, :], r1[:, 2, :]))
            link(V.tensor_tensor(r1[:, 5, :], r1[:, 4, :], r1[:, 3, :], ALU.mult))
            def expert_lo(done, u):
                cols = UNITS[u % M_UNITS][3]
                V.wait_ge(m_hi_ready, done + (u + 1))
                V.tensor_tensor(m_lo[:, u % M_SPL, 0:cols], m_raw[:, u % M_RAW, 0:cols],
                                m_hi[:, u % M_SPL, 0:cols].bitcast(F32), ALU.subtract).then_inc(m_lo_ready, 1)

            def turned_x(done, sl):
                for hb in range(2):
                    k = slice(4 * hb, 4 * hb + 4)
                    V.wait_ge(xt_hi_ready, done + (2 * sl + hb + 1))
                    lo_of(xt_lo[:, k, sl, :], ps[:, hb, :].rearrange("p (k c) -> p k c", c=P),
                          xt_hi[:, k, sl, :]).then_inc(xt_lo_ready, 1)

            for u in range(M_SPL):
                expert_lo(0, u)
            turned_x(0, 0)
            turned_x(0, 1)

            def passes(first, always_both):
                with V.Fori(0, N_SEC) as i:
                    def pass_of(slots):
                        for u in range(M_UNITS):
                            for c in range(len(CHUNKS)):
                                if u == CHUNK_END[c]["up"]:
                                    w = CHUNKS[c] * P
                                    V.wait_ge(m_done, i * M_UNITS + (first * M_UNITS + u + 1))
                                    for sl in range(slots):
                                        V.wait_ge(m_silu_ready, i * 6 + (6 * first + SLOTS + 2 * c + sl + 1))
                                        V.wait_ge(at_turned, i * 6 + (6 * first + 2 * c + sl + 1))
                                        V.tensor_tensor(m_act[:, sl, 0:w], m_silu[:, sl, 0:w], ps[:, 2 + sl, 0:w],
                                                        ALU.mult).then_inc(m_act_ready, SLOTS // slots)
                            expert_lo(i * M_UNITS + first * M_UNITS, u + M_SPL)
                            if u in TURNED_AT:
                                c = TURNED_AT[u]
                                nb = CHUNKS[c]
                                for sl in range(slots):
                                    V.wait_ge(at_hi_ready, i * 6 + (6 * first + 2 * c + sl + 1))
                                    lo_of(at_lo[:, 4 * c:4 * c + nb, sl, :], ps[:, 4 + sl, 0:nb * P].rearrange("p (k c) -> p k c", c=P),
                                          at_hi[:, 4 * c:4 * c + nb, sl, :]).then_inc(at_lo_ready, SLOTS // slots)
                            if u in TURN_X:
                                turned_x(i * 4 + 4 * (first + 1), TURN_X.index(u))

                    if always_both:
                        pass_of(SLOTS)
                    else:
                        with V.If(V.value_load(counts[0:1, bass.ds(i, 1)], min_val=0, max_val=T) > P):
                            pass_of(SLOTS)
                        with V.Else():
                            pass_of(1)

            passes(0, False)
            with V.If(V.value_load(most[0:1, 0:1], min_val=0, max_val=T) > CAP):
                passes(N_SEC, True)
            V.wait_ge(rows_in, 32)
            for t in range(TT + 1):
                if t < TT:
                    V.wait_ge(y_back[t], 16)
                    V.scalar_tensor_tensor(out=x_rows[:, t, :], in0=y_of(t)[:, 0, :], scalar=r1[:, 4, t:t + 1],
                                           in1=x_rows[:, t, :], op0=ALU.mult, op1=ALU.add).then_inc(mix_step, 1)
                    V.wait_ge(mix_step, t + 1)
                    V.scalar_tensor_tensor(out=x_rows[:, t, :], in0=y_of(t)[:, 1, :], scalar=r1[:, 5, t:t + 1],
                                           in1=x_rows[:, t, :], op0=ALU.mult, op1=ALU.add).then_inc(mixed, 1)
                if t >= 1:
                    V.wait_ge(root_ready, t)
                    V.reciprocal(r1[:, 6, t - 1:t], r1[:, 9, t - 1:t]).then_inc(inv_ready, 1)
                if t >= 3:
                    V.wait_ge(inv_ready, t)
                    V.scalar_tensor_tensor(out=x_rows[:, t - 1, :], in0=x_rows[:, t - 1, :], scalar=r1[:, 6, t - 1:t],
                                           in1=gf_row, op0=ALU.mult, op1=ALU.mult).then_inc(dve_out, 1)

        @block.tensor
        def _(E):
            def unit_ready(n):
                E.wait_ge(lo_ready, n + 1)

            def tile_products(n, i, bank, hi, lo, first, final):
                wh, wl = split_of(n, i * P, (i + 1) * P)
                E.matmul(ps[:, bank, :], wh, hi, start=first, stop=False)
                E.matmul(ps[:, bank, :], wh, lo, start=False, stop=False)
                return E.matmul(ps[:, bank, :], wl, hi, start=False, stop=final)

            def keep_warm(n):
                for _ in range(n):
                    E.matmul(ps[:, IDLE_BANK, :], idle[:], idle[:].unsqueeze(1).to_broadcast([P, TT, P]), start=True, stop=True)

            def turn_x(t):
                if t:
                    E.wait_ge(x_copied, t)
                for k in range(KD):
                    tr = E.transpose(ps[:, k // 4, (k % 4) * P:(k % 4 + 1) * P], xs[:, k, t * P:(t + 1) * P], ident[:])
                tr.then_inc(x_turned, 1)

            def mean_square(j):
                if j == 0:
                    E.wait_ge(summed, 3)
                keep_warm(16)
                E.wait_ge(summed, (j + 1) * KD)
                for t in range(TT):
                    mm = E.matmul(ps[:, SUM_BANK, t:t + 1], norm[:, t * P:(t + 1) * P], mean_of[:], start=True, stop=True)
                mm.then_inc(mean_ready, 1)
                if j == 3:
                    turn_x(0)
                else:
                    keep_warm(4)
                E.wait_ge(diag_ready, j + 1)
                E.matmul(ps[:, SUM_BANK, :], ones[:], norm[:], start=True, stop=True).then_inc(rinv_spread, 1)
                if j == 3:
                    turn_x(1)
                    keep_warm(4)
                else:
                    keep_warm(9)

            def x_unit(n, bank):
                unit_ready(n)
                for k in range(KD):
                    mm = tile_products(n, k, bank, h_hi[:, k, :], h_lo[:, k, :], k == 0, k == KD - 1)
                return mm

            def first_units(n, j):
                unit_ready(n + 1)
                for k in range(KD):
                    E.wait_ge(h_lo_ready, j * KD + k + 1)
                    for v in (n, n + 1):
                        mm = tile_products(v, k, v % 2, h_hi[:, k, :], h_lo[:, k, :], k == 0, k == KD - 1)
                        if k == KD - 1:
                            mm.then_inc(unit_done, 1)

            def turn_v(layer, u):
                i = layer * N_V + u
                E.wait_ge(vT_copied, i + 1)
                if i >= 2:
                    E.wait_ge(v_lo_ready, i - 1)
                for t in range(TT):
                    tr = E.transpose(ps[:, T_BANK + i % 2, t * P:(t + 1) * P], probs[:, i % 2, t * P:(t + 1) * P], ident[:])
                tr.then_inc(vT_turned, 1)

            E.wait_ge(basics, 3)
            mean_square(0)
            for layer in range(DEPTH):
                n0 = MIX_START[layer]
                norm_i = 2 * layer
                dve0 = layer * N_PROJ
                first_units(n0, norm_i)
                for u in range(2, N_PROJ):
                    n = n0 + u
                    E.wait_ge(drained_dve, dve0 + u - 1)
                    unit_ready(n)
                    for k in range(KD):
                        mm = tile_products(n, k, n % 2, h_hi[:, k, :], h_lo[:, k, :], k == 0, k == KD - 1)
                    mm.then_inc(unit_done, 1)
                for u in range(N_V + 1):
                    n = n0 + U_V + u
                    if u < N_V:
                        if u < 2:
                            E.wait_ge(drained_dve, dve0 + N_PROJ - 1 + u)
                        else:
                            E.wait_ge(vT_copied, layer * N_V + u - 1)
                        x_unit(n, n % 2).then_inc(unit_done, 1)
                    if u >= 1:
                        turn_v(layer, u - 1)
                E.wait_ge(v_lo_ready, layer * N_V + N_V)
                E.wait_ge(drained_dve, dve0 + N_PROJ)
                E.wait_ge(flip_ready, 1)

                for tick in range(STEPS + 4):
                    def gate_part(half):
                        g = tick // 4
                        n = n0 + U_GATE + g
                        if tick % 4 == 0 and half == 0:
                            unit_ready(n)
                            if g < 2:
                                E.wait_ge(vT_copied, layer * N_V + N_V - 1 + g)
                            else:
                                E.wait_ge(drained_act, layer * N_GATE + g - 1)
                        k = 2 * (tick % 4) + half
                        mm = tile_products(n, k, n % 2, h_hi[:, k, :], h_lo[:, k, :], k == 0, k == KD - 1)
                        if k == KD - 1:
                            mm.then_inc(unit_done, 1)

                    if 2 <= tick < STEPS + 2:
                        s, st = layer * STEPS + tick - 2, step(tick - 2)
                        E.wait_ge(probs_ready, s + 1)
                        if s >= 2:
                            E.wait_ge(pT_lo_ready, s - 1)
                        for b in range(st["nk"] // P):
                            tr = E.transpose(ps[:, T_BANK + s % 2, b * P:(b + 1) * P], probs[:, s % 2, b * P:(b + 1) * P], ident[:])
                        tr.then_inc(pT_ready, 1)
                    if tick < STEPS:
                        s, st = layer * STEPS + tick, step(tick)
                        r, k0, nk, qb = st["rows"], st["k0"], st["nk"], st["qb"]
                        H = layer * 2 * HEADS + st["hh"]
                        if s >= 2:
                            E.wait_ge(exp_ready, s - 1)
                        near = min(nk, 2 * P)
                        out = ps[:, S_BANK + s % 2, 0:nk]
                        q_hi = kq_hi[r:r + HD, st["q"], qb * P:(qb + 1) * P]
                        q_lo = kq_lo[r:r + HD, st["q"], qb * P:(qb + 1) * P]
                        k_hi = kq_hi[r:r + HD, st["k"], k0:k0 + nk]
                        k_lo = kq_lo[r:r + HD, st["k"], k0:k0 + nk]
                        E.matmul(out, q_hi, k_hi, start=True, stop=False)
                        E.wait_ge(bias_hi_ready, H + 1)
                        E.matmul(out[:, nk - near:nk], flip_r[:], bias_hi[:, H % 2, 2 * P - near:2 * P], start=False, stop=False)
                        if st["a"]:
                            E.wait_ge(bias_lo_ready, layer * HEADS + st["hh"] + 1)
                            E.matmul(out[:, nk - near:nk], flip_r[:], bias_lo[:, H % 2, 2 * P - near:2 * P], start=False, stop=False)
                        E.matmul(out, q_hi, k_lo, start=False, stop=False)
                        E.matmul(out, q_lo, k_hi, start=False, stop=True).then_inc(scores_ready, 1)
                        gate_part(0)
                    if 4 <= tick:
                        pair, half = (tick - 4) // 2, tick % 2
                        p = layer * STEPS // 2 + pair
                        hh = pair // 2
                        v = step(2 * pair)["v"]
                        products = pair_products(pair)
                        if half == 0:
                            E.wait_ge(pT_lo_ready, 2 * p + 2)
                            if pair % 2 == 0 and hh >= 2:
                                E.wait_ge(y_lo_ready, layer * 2 * HEADS + hh - 1)
                        vc = slice(v * P, (v + 1) * P)
                        for j, (kt, b, q, nq) in enumerate(products):
                            if (j >= len(products) // 2) == (half == 1):
                                out = ps[:, O_BANK + hh % 2, q * P:(q + nq) * P]
                                p_hi, p_lo = (part[:, b:b + nq, :].rearrange("p b c -> p (b c)") for part in (pT_hi, pT_lo))
                                E.matmul(out, v_hi[:, kt, vc], p_hi, start=j == 0, stop=False)
                                E.matmul(out, v_hi[:, kt, vc], p_lo, start=False, stop=False)
                                mm = E.matmul(out, v_lo[:, kt, vc], p_hi, start=False, stop=j == len(products) - 1)
                        if half == 1:
                            mm.then_inc(pv_done, 1)
                    if tick < STEPS:
                        gate_part(1)

                E.wait_ge(y_lo_ready, (layer + 1) * 2 * HEADS)
                E.wait_ge(drained_act, (layer + 1) * N_GATE)
                for i in range(N_BR // 2):
                    if i >= 2:
                        E.wait_ge(merged_lo, layer * KD + 2 * (i - 1))
                    for which, bank in enumerate(branch_banks(i)):
                        n = n0 + U_BR + 2 * i + which
                        unit_ready(n)
                        for mm_ in range(2):
                            for k in range(4):
                                y = 4 + 4 * which + k
                                mm = tile_products(n, 4 * mm_ + k, bank + mm_, kq_hi[:, y, :], kq_lo[:, y, :], k == 0, k == 3)
                        mm.then_inc(unit_done, 1)
                for u in range(N_OUT):
                    n = n0 + U_OUT + u
                    unit_ready(n)
                    if u >= 2:
                        E.wait_ge(x_updated, 2 * layer * KD + u - 1)
                    if u == 0:
                        E.wait_ge(merged_lo, layer * KD + KD - 2)
                    for k in range(KD):
                        if u == 0 and k >= KD - 2:
                            E.wait_ge(merged_lo, layer * KD + k + 1)
                        mm = tile_products(n, k, T_BANK + n % 2, h_hi[:, k, :], h_lo[:, k, :], k == 0, k == KD - 1)
                    mm.then_inc(unit_done, 1)
                mean_square(norm_i + 1)
                if layer == 0:
                    E.wait_ge(x_updated, KD)
                    first_units(FFN_START, 1)
                    for u in range(2, N_GU):
                        n = FFN_START + u
                        unit_ready(n)
                        f = u // 2
                        if u % 2 == 0:
                            E.wait_ge(silu_ready, f)
                        else:
                            E.wait_ge(act_ready, f)
                        for k in range(KD):
                            mm = tile_products(n, k, n % 2, h_hi[:, k, :], h_lo[:, k, :], k == 0, k == KD - 1)
                        mm.then_inc(unit_done, 1)
                    E.wait_ge(act_ready, KF)
                    for u in range(N_DOWN):
                        n = FFN_START + N_GU + u
                        m, part = u // 3, u % 3
                        unit_ready(n)
                        if part == 0 and m >= 2:
                            E.wait_ge(x_updated, KD + m - 1)
                        for t in range(DOWN_TILES[part]):
                            f = 8 * part + t
                            if m == 0:
                                E.wait_ge(a_lo_ready, f + 1)
                            mm = tile_products(n, t, m % 2, a_hi[:, f, :], a_lo[:, f, :], f == 0, f == KF - 1)
                        mm.then_inc(unit_done, 1)
                    mean_square(2)

            E.sem_inc(at_turned, SLOTS)
            unit_ready(U_ROUTER)
            for k in range(KD):
                E.wait_ge(h_lo_ready, 3 * KD + k + 1)
                mm = tile_products(U_ROUTER, k, 3, h_hi[:, k, :], h_lo[:, k, :], k == 0, k == KD - 1)
                if k in (1, 3):
                    turn_x((k + 3) // 2)
            mm.then_inc(unit_done, 1)
            keep_warm(3)
            E.wait_ge(logits_ready, 1)
            for t in range(TT):
                tr = E.transpose(ps[:, 2, t * P:(t + 1) * P], logits_T[:, t * P:(t + 1) * P], ident[:])
            tr.then_inc(logits_turned, 1)
            keep_warm(12)
            E.wait_ge(picks_ready, 1)
            for t in range(TT):
                for b in range(t + 1):
                    E.matmul(ps[:, 3, t * EXPERTS:(t + 1) * EXPERTS], before[:] if b == t else all_ones[:], picks[:, b, :],
                             start=b == 0, stop=b == t)
            for b in range(TT):
                mm = E.matmul(ps[:, 3, 64:64 + EXPERTS], all_ones[:], picks[:, b, :], start=b == 0, stop=b == TT - 1)
            mm.then_inc(ranks_ready, 1)
            keep_warm(12)
            for j in range(2 * TT):
                E.wait_ge(places_ready, j // TT + 1)
                mm = E.matmul(ps[:, 2, 0:2 * LISTS], row_hit[:, j, :], entry_hit[:, j, :, :].rearrange("p c i -> p (c i)"),
                              start=j == 0, stop=j == 2 * TT - 1)
            mm.then_inc(lists_summed, 1)
            E.wait_ge(counts_ready, 1)
            E.wait_ge(x_copied, TT)

            def turn_rows(done, sl, p16):
                E.wait_ge(xg_in[sl], p16)
                for k in range(KD):
                    if sl and k % 4 == 0:
                        E.wait_ge(xt_lo_ready, done + (k // 4 + 1))
                    tr = E.transpose(ps[:, k // 4, (k % 4) * P:(k % 4 + 1) * P], xg[:, sl, k * P:(k + 1) * P], ident[:])
                    if k % 4 == 3:
                        tr.then_inc(xt_turned, 1)

            keep_warm(24)
            turn_rows(0, 0, 16)
            turn_rows(0, 1, 16)

            def passes(first, always_both):
                with E.Fori(0, N_SEC) as i:
                    def pass_of(slots):
                        def three(out, a_hi_, a_lo_, u, lo_col, n, start, stop):
                            wh, wl = m_hi[:, u % M_SPL, lo_col:lo_col + n], m_lo[:, u % M_SPL, lo_col:lo_col + n]
                            E.matmul(out, a_hi_, wh, start=start, stop=False)
                            E.matmul(out, a_hi_, wl, start=False, stop=False)
                            return E.matmul(out, a_lo_, wh, start=False, stop=stop)

                        def turn_act(c):
                            for sl in range(SLOTS):
                                E.wait_ge(m_act_ready, i * 6 + (6 * first + SLOTS + 2 * c + sl + 1))
                                E.wait_ge(at_lo_ready, i * 6 + (6 * first + 2 * c + sl + 1))
                                if sl < slots:
                                    for b in range(CHUNKS[c]):
                                        tr = E.transpose(ps[:, 4 + sl, b * P:(b + 1) * P], m_act[:, sl, b * P:(b + 1) * P], ident[:])
                                    tr.then_inc(at_turned, 1)
                                else:
                                    E.wait_ge(at_turned, i * 6 + (6 * first + SLOTS + 2 * c + sl))
                                    E.sem_inc(at_turned, 1)

                        E.wait_ge(xt_lo_ready, i * 4 + (4 * first + 4))
                        for u, (what, c, j, cols) in enumerate(UNITS):
                            w = cols // 2
                            E.wait_ge(m_lo_ready, i * M_UNITS + (first * M_UNITS + u + 1))
                            if what != "down":
                                if j == 0 and c:
                                    E.wait_ge(m_silu_ready if what == "gate" else m_act_ready, i * 6 + (6 * first + SLOTS + 2 * c))
                                if j == 0 and not c and what == "up":
                                    E.wait_ge(y_copied, i * SLOTS + (SLOTS * first + SLOTS))
                                for sl in range(slots):
                                    for k in (2 * j, 2 * j + 1):
                                        mm = three(ps[:, (0 if what == "gate" else 2) + sl, 0:w], xt_hi[:, k, sl, :],
                                                   xt_lo[:, k, sl, :], u, (k % 2) * w, w, k == 0, k == KD - 1)
                                mm.then_inc(m_done, 1)
                                if c and what == "gate" and j == 0:
                                    turn_act(c - 1)
                            else:
                                f = j
                                for sl in range(slots):
                                    if f == 0 and sl:
                                        E.wait_ge(m_act_ready, i * 6 + (6 * first + SLOTS + 2 * len(CHUNKS)))
                                    if f % 4 == 0:
                                        E.wait_ge(at_lo_ready, i * 6 + (6 * first + SLOTS + 2 * (f // 4) + sl + 1))
                                    for half in range(2):
                                        mm = three(ps[:, Y_BANKS[sl] + half, :], at_hi[:, f, sl, :], at_lo[:, f, sl, :], u,
                                                   half * T, T, f == 0, f == KFE - 1)
                                mm.then_inc(m_done, 1)
                                if u == TURN_LAST:
                                    turn_act(2)
                                if u in TURN_X:
                                    if u == TURN_X[0]:
                                        E.wait_ge(m_silu_ready, i * 6 + (6 * first + SLOTS + 2 * len(CHUNKS)))
                                    turn_rows(i * 4 + 4 * (first + 1), TURN_X.index(u), i * 16 + 16 * (first + 2))

                    if always_both:
                        pass_of(SLOTS)
                    else:
                        with E.If(E.value_load(counts[0:1, bass.ds(i, 1)], min_val=0, max_val=T) > P):
                            pass_of(SLOTS)
                        with E.Else():
                            pass_of(1)

            passes(0, False)
            with E.If(E.value_load(most[0:1, 0:1], min_val=0, max_val=T) > CAP):
                passes(N_SEC, True)


def host_layout(i):
    import numpy as np
    f = lambda a: np.ascontiguousarray(a)
    x = np.asarray(i["x"])[0]
    A, Bw = 512, 512
    w_in = np.asarray(i["w_in"])
    o = np.cumsum([0, 512, 512, 512, 512, 128, 128, 2048])
    cols = lambda a, n: np.arange(a, a + n)
    cb = np.concatenate([cols(64 * (j + 4 * g), 64) for j in range(4) for g in range(2)])
    gate_cols = np.concatenate([cols(o[6] + g * 1024 + m * 128, 128) for m in range(8) for g in range(2)])
    order = np.concatenate([cols(o[1], 512), cols(o[0], 512), o[3] + cb, cols(o[4], 128), cols(o[2], 512), cols(o[5], 128), gate_cols])
    units = lambda w, k, per: w.reshape(k, 128, -1, per, 128).transpose(2, 1, 3, 0, 4).reshape(-1, 128, per * k * 128)
    both = lambda fn, w: f(np.stack([fn(np.asarray(w)[l]) for l in range(2)]))
    rb = np.asarray(i["rel_bias"])
    rev = rb[:, :, ::-1][:, :, :256]
    ext = np.concatenate([np.repeat(rev[:, :, :1], 127, axis=2), rev, rev[:, :, -1:]], axis=2)
    pk = lambda g: np.asarray(g).reshape(-1, 8, 128).transpose(2, 0, 1)
    bgt = np.asarray(i["b_gate"]).reshape(2, 2, 8, 128).transpose(3, 0, 2, 1).reshape(128, 2, 16)
    gu = np.stack([np.asarray(i["ffn_w_gate"])[0].reshape(1024, 22, 128), np.asarray(i["ffn_w_up"])[0].reshape(1024, 22, 128)], axis=2).reshape(1024, -1)
    dn = np.asarray(i["ffn_w_down"])[0]
    wr = np.zeros((1024, 128), np.float32)
    wr[:, :8] = np.asarray(i["w_router"])[0]
    wr = wr.reshape(8, 128, 128).transpose(1, 0, 2).reshape(128, 1024)
    def chunk(w, a, n):
        return w[:, :, a:a + n].reshape(8, 4, 2, 128, n).transpose(0, 1, 3, 2, 4).reshape(8, 4, 128, 2 * n)
    g, u = np.asarray(i["moe_w_gate"])[0], np.asarray(i["moe_w_up"])[0]
    mgu = (np.stack([np.concatenate([chunk(g, a, 512), chunk(u, a, 512)], axis=1) for a in (0, 512)]),
           np.concatenate([chunk(g, 1024, 384), chunk(u, 1024, 384)], axis=1))
    return dict(
        xT=f(x.T.reshape(8, 128, 512).transpose(1, 0, 2)),
        g_mix=f(pk(i["norm_mix"])), w_in=both(lambda w: units(w[:, order], 8, 1), w_in), b_gate=f(bgt),
        rel_ext=f(ext), sinks=f(np.asarray(i["sinks"])),
        w_a=both(lambda w: units(w, 4, 2), i["w_branch_a"]),
        w_b=both(lambda w: units(w[cb], 4, 2), i["w_branch_b"]),
        w_out=both(lambda w: units(w, 8, 1), i["w_out"]),
        g_ffn=f(pk(i["norm_ffn"])), w_gu=f(units(gu, 8, 1)), w_down=f(units(dn, 22, 1)),
        w_router=f(wr), moe_g01=f(mgu[0]), moe_g2=f(mgu[1]),
        moe_down=f(np.asarray(i["moe_w_down"])[0].reshape(8, 11, 128, 1024)),
        g_ffn_row=f(np.asarray(i["norm_ffn"])[1:2]), g_final_row=f(np.asarray(i["norm_final"])[None]),
    )


_OUT = (T, D)


def kernel(**inputs):
    import concourse.bacc as _bacc
    import numpy as _np
    from concourse import mybir as _mybir
    from concourse.bass_utils import run_bass_kernel_spmd as _run

    nc = _bacc.Bacc("TRN2", target_bir_lowering=False, num_devices=1)
    arrays = host_layout(inputs)
    ap = {n: nc.dram_tensor(n, a.shape, _mybir.dt.from_np(a.dtype), kind="ExternalInput").ap() for n, a in arrays.items()}
    out = nc.dram_tensor("out", _OUT, F32, kind="ExternalOutput").ap()
    moe_gu = (ap.pop("moe_g01"), ap.pop("moe_g2"))
    build_kernel(nc, moe_gu=(moe_gu[0][0], moe_gu[0][1], moe_gu[1]), out=out, **ap)
    r = _run(nc, [arrays], core_ids=[0])
    return _np.asarray(r.results[0]["out"]).reshape(1, *_OUT)
```
